# Optimizing a Trainium2 kernel written in Bass

```python
import jax, jax.numpy as jnp
from jax import lax
import numpy as np

D_MODEL = 1024
BATCH = 1
SEQ = 512
DEPTH = 1
DEC_BATCH = 8
DEC_SEQ = 4
PAST_LEN = 2048
PAGE_SIZE = 128

GLA_WIDTH = D_MODEL // 2
SWA_WIDTH = D_MODEL - GLA_WIDTH
GLA_HEADS = 4
GLA_DV = GLA_WIDTH // GLA_HEADS
GLA_DK = GLA_DV // 2
GLA_QK = GLA_HEADS * GLA_DK
GLA_GATE_RANK = 16
GLA_GATE_NORM = 16.0
GLA_CHUNK = 64
HEAD_DIM = 64
SWA_HEADS = SWA_WIDTH // HEAD_DIM
SWA_KV_HEADS = 2
SWA_GROUP = SWA_HEADS // SWA_KV_HEADS
WINDOW = 128
ROPE_DIM = HEAD_DIM // 4
ROPE_THETA = 500000.0
N_EXPERTS = 32
TOP_K = 4
EXPERT_DFF = D_MODEL
MOE_BLOCK = 128
SWIGLU_LIMIT = 7.0
SWIGLU_ALPHA = 1.702
NORM_EPS = 1e-5
DEEPNORM_ALPHA = (2 * DEPTH) ** 0.25
DEEPNORM_BETA = (8 * DEPTH) ** -0.25
IN_SPLITS = (GLA_QK, GLA_QK, GLA_WIDTH, GLA_WIDTH, GLA_GATE_RANK,
             SWA_HEADS * HEAD_DIM, SWA_KV_HEADS * HEAD_DIM, SWA_KV_HEADS * HEAD_DIM)
D_IN = sum(IN_SPLITS)

kernel_name = 'hymba_gla_swa_sink_moe_deepnorm_step'

def layer_norm(x, g, b):
    xf = x.astype(jnp.float32)
    mu = xf.mean(-1, keepdims=True)
    var = jnp.square(xf - mu).mean(-1, keepdims=True)
    return ((xf - mu) * lax.rsqrt(var + NORM_EPS) * g.astype(jnp.float32)
            + b.astype(jnp.float32)).astype(x.dtype)

def rms_norm_f32(x, g):
    xf = x.astype(jnp.float32)
    return xf * lax.rsqrt(jnp.mean(xf * xf, -1, keepdims=True) + NORM_EPS) * g.astype(jnp.float32)

def rope_partial(x, pos):
    half = ROPE_DIM // 2
    freqs = ROPE_THETA ** (-jnp.arange(half, dtype=jnp.float32) * 2.0 / ROPE_DIM)
    ang = pos.astype(jnp.float32)[:, None] * freqs[None, :]
    cos = jnp.cos(ang)[:, None, :].astype(x.dtype)
    sin = jnp.sin(ang)[:, None, :].astype(x.dtype)
    x1 = x[..., :half]
    x2 = x[..., half:ROPE_DIM]
    return jnp.concatenate([x1 * cos - x2 * sin, x2 * cos + x1 * sin, x[..., ROPE_DIM:]], axis=-1)

def gla_recurrence(q, k, v, gk, s0):
    B, L, H, _ = q.shape
    C = min(GLA_CHUNK, L)
    n = -(-L // C)
    pad = n * C - L

    def blocks(t):
        t = jnp.pad(t.astype(jnp.float32), ((0, 0), (0, pad), (0, 0), (0, 0)))
        return t.reshape(B, n, C, H, t.shape[-1]).transpose(1, 0, 3, 2, 4)

    causal = jnp.tril(jnp.ones((C, C), dtype=bool))

    def step(S, inp):
        qi, ki, vi, gi = inp
        b = jnp.cumsum(gi, axis=2)
        b_last = b[:, :, -1:, :]
        o_inter = jnp.einsum('bhtd,bhde->bhte', qi * jnp.exp(b), S)
        diff = jnp.where(causal[:, :, None], b[:, :, :, None, :] - b[:, :, None, :, :], -jnp.inf)
        att = jnp.einsum('bhtd,bhtsd,bhsd->bhts', qi, jnp.exp(diff), ki)
        o = o_inter + jnp.einsum('bhts,bhse->bhte', att, vi)
        S = S * jnp.exp(b_last[:, :, 0, :, None]) + jnp.einsum(
            'bhsd,bhse->bhde', ki * jnp.exp(b_last - b), vi)
        return S, o

    S, o = lax.scan(step, s0.astype(jnp.float32), (blocks(q), blocks(k), blocks(v), blocks(gk)))
    o = o.transpose(1, 0, 3, 2, 4).reshape(B, n * C, H, v.shape[-1])[:, :L]
    return o, S

def sink_attention(q, k, v, mask, sinks):
    s = jnp.einsum('bnqhgd,bnkhd->bnhgqk', q, k).astype(jnp.float32) * (HEAD_DIM ** -0.5)
    s = jnp.where(mask[None, :, None, None], s, -jnp.inf)
    sink = sinks.astype(jnp.float32)[None, None, :, :, None, None]
    m = jnp.maximum(s.max(-1, keepdims=True), sink)
    p = jnp.exp(s - m)
    p = (p / (p.sum(-1, keepdims=True) + jnp.exp(sink - m))).astype(v.dtype)
    return jnp.einsum('bnhgqk,bnkhd->bnqhgd', p, v)

def swa_prompt(q, k, v, sinks):
    B, S = q.shape[:2]
    n = S // WINDOW
    qb = q.reshape(B, n, WINDOW, SWA_KV_HEADS, SWA_GROUP, HEAD_DIM)

    def band(t):
        tp = jnp.pad(t, ((0, 0), (WINDOW, 0), (0, 0), (0, 0))).reshape(B, n + 1, WINDOW, SWA_KV_HEADS, HEAD_DIM)
        return jnp.concatenate([tp[:, :-1], tp[:, 1:]], axis=2)

    qpos = jnp.arange(S).reshape(n, WINDOW)
    kpos = jnp.arange(n)[:, None] * WINDOW - WINDOW + jnp.arange(2 * WINDOW)[None, :]
    d = qpos[:, :, None] - kpos[:, None, :]
    mask = (d >= 0) & (d < WINDOW) & (kpos[:, None, :] >= 0)
    o = sink_attention(qb, band(k), band(v), mask, sinks)
    return o.reshape(B, S, SWA_WIDTH), k[:, -WINDOW:], v[:, -WINDOW:]

def swa_sample(q, k, v, k_buf, v_buf, pos, sinks):
    B, L = q.shape[:2]
    W = k_buf.shape[1]
    kk = jnp.concatenate([k_buf.astype(k.dtype), k], axis=1)
    vv = jnp.concatenate([v_buf.astype(v.dtype), v], axis=1)
    kpos = jnp.concatenate([pos[0] - W + jnp.arange(W), pos])
    d = pos[:, None] - kpos[None, :]
    mask = ((d >= 0) & (d < WINDOW) & (kpos[None, :] >= 0))[None]
    o = sink_attention(q.reshape(B, 1, L, SWA_KV_HEADS, SWA_GROUP, HEAD_DIM),
                       kk[:, None], vv[:, None], mask, sinks)
    return o.reshape(B, L, SWA_WIDTH), kk[:, -W:], vv[:, -W:]

def clamped_swiglu(gate, up):
    gate = jnp.minimum(gate, SWIGLU_LIMIT)
    up = jnp.clip(up, -SWIGLU_LIMIT, SWIGLU_LIMIT)
    return gate * jax.nn.sigmoid(SWIGLU_ALPHA * gate) * (up + 1.0)

def moe_ffn(x, w_router, b_router, w_gate, b_gate, w_up, b_up, w_down, b_down):
    shp = x.shape
    xt = x.reshape(-1, D_MODEL)
    T = xt.shape[0]
    logits = (xt @ w_router + b_router).astype(jnp.float32)
    top_val, top_idx = lax.top_k(logits, TOP_K)
    gate_w = jax.nn.softmax(top_val, axis=-1)
    A = T * TOP_K
    flat_e = top_idx.reshape(-1)
    order = jnp.argsort(flat_e)
    sorted_e = flat_e[order]
    token_of = order // TOP_K
    counts = jnp.bincount(flat_e, length=N_EXPERTS)
    padded = (counts + MOE_BLOCK - 1) // MOE_BLOCK * MOE_BLOCK
    pad_end = jnp.cumsum(padded)
    pad_start = pad_end - padded
    start = jnp.cumsum(counts) - counts
    dest = pad_start[sorted_e] + jnp.arange(A) - start[sorted_e]
    n_blocks = -(-A // MOE_BLOCK) + N_EXPERTS
    slot_token = jnp.full((n_blocks * MOE_BLOCK,), T, jnp.int32).at[dest].set(token_of)
    block_expert = jnp.minimum(
        jnp.searchsorted(pad_end, jnp.arange(n_blocks) * MOE_BLOCK, side='right'), N_EXPERTS - 1)
    x_pad = jnp.concatenate([xt, jnp.zeros((1, D_MODEL), xt.dtype)], axis=0)
    xb = x_pad[slot_token].reshape(n_blocks, MOE_BLOCK, D_MODEL)

    def expert_block(args):
        xe, e = args
        h = clamped_swiglu(xe @ w_gate[e] + b_gate[e], xe @ w_up[e] + b_up[e])
        return h @ w_down[e] + b_down[e]

    yb = lax.map(expert_block, (xb, block_expert)).reshape(n_blocks * MOE_BLOCK, D_MODEL)
    y_assign = yb[dest] * gate_w.reshape(-1)[order][:, None].astype(xt.dtype)
    out = jnp.zeros_like(xt).at[token_of].add(y_assign)
    return out.reshape(shp)

def decoder_layer(x, pos, gla_s0, swa_k_buf, swa_v_buf, w_in, w_gk_up, b_gk_up, gla_norm_g,
                  swa_sinks, w_out, ln1_g, ln1_b, w_router, b_router, w_gate, b_gate,
                  w_up, b_up, w_down, b_down, ln2_g, ln2_b):
    B, L, _ = x.shape
    h = x @ w_in
    q_g, k_g, v_g, o_gate, g_lr, q_s, k_s, v_s = jnp.split(
        h, np.cumsum(IN_SPLITS)[:-1].tolist(), axis=-1)
    gk = jax.nn.log_sigmoid((g_lr @ w_gk_up + b_gk_up).astype(jnp.float32)) / GLA_GATE_NORM
    o_gla, s_new = gla_recurrence(
        q_g.reshape(B, L, GLA_HEADS, GLA_DK) * (GLA_DK ** -0.5),
        k_g.reshape(B, L, GLA_HEADS, GLA_DK),
        v_g.reshape(B, L, GLA_HEADS, GLA_DV),
        gk.reshape(B, L, GLA_HEADS, GLA_DK), gla_s0)
    o_gla = rms_norm_f32(o_gla, gla_norm_g) * jax.nn.silu(
        o_gate.reshape(B, L, GLA_HEADS, GLA_DV).astype(jnp.float32))
    o_gla = o_gla.reshape(B, L, GLA_WIDTH).astype(x.dtype)
    q = rope_partial(q_s.reshape(B, L, SWA_HEADS, HEAD_DIM), pos)
    k = rope_partial(k_s.reshape(B, L, SWA_KV_HEADS, HEAD_DIM), pos)
    v = v_s.reshape(B, L, SWA_KV_HEADS, HEAD_DIM)
    sinks = swa_sinks.reshape(SWA_KV_HEADS, SWA_GROUP)
    if swa_k_buf is None:
        o_swa, k_keep, v_keep = swa_prompt(q, k, v, sinks)
    else:
        o_swa, k_keep, v_keep = swa_sample(q, k, v, swa_k_buf, swa_v_buf, pos, sinks)
    mix = jnp.concatenate([o_gla, o_swa], axis=-1) @ w_out
    x1 = layer_norm(DEEPNORM_ALPHA * x + mix, ln1_g, ln1_b)
    ffn = moe_ffn(x1, w_router, b_router, w_gate, b_gate, w_up, b_up, w_down, b_down)
    x2 = layer_norm(DEEPNORM_ALPHA * x1 + ffn, ln2_g, ln2_b)
    return x2, s_new.astype(x.dtype), k_keep, v_keep

def setup_inputs(seed: int = 0) -> dict:
    key = jax.random.key(seed)
    ks = jax.random.split(key, 24)
    nrm = lambda i, shape, scale: jax.random.normal(ks[i], shape, jnp.float32) * scale
    return {
        'x_prompt': nrm(0, (BATCH, SEQ, D_MODEL), 1.0),
        'x_sample': nrm(1, (DEC_BATCH, DEC_SEQ, D_MODEL), 1.0),
        'state_gla': nrm(2, (DEPTH, DEC_BATCH, GLA_HEADS, GLA_DK, GLA_DV), 0.5),
        'cache_swa_k': nrm(3, (DEPTH, DEC_BATCH, WINDOW, SWA_KV_HEADS, HEAD_DIM), 1.0),
        'cache_swa_v': nrm(4, (DEPTH, DEC_BATCH, WINDOW, SWA_KV_HEADS, HEAD_DIM), 1.0),
        'w_in': nrm(5, (DEPTH, D_MODEL, D_IN), D_MODEL ** -0.5),
        'w_gk_up': nrm(6, (DEPTH, GLA_GATE_RANK, GLA_QK), GLA_GATE_RANK ** -0.5),
        'b_gk_up': nrm(7, (DEPTH, GLA_QK), 0.1),
        'gla_norm_g': 1.0 + nrm(8, (DEPTH, GLA_DV), 0.02),
        'swa_sinks': nrm(9, (DEPTH, SWA_HEADS), 1.0),
        'w_out': nrm(10, (DEPTH, D_MODEL, D_MODEL), DEEPNORM_BETA * D_MODEL ** -0.5),
        'ln1_g': 1.0 + nrm(11, (DEPTH, D_MODEL), 0.02),
        'ln1_b': nrm(12, (DEPTH, D_MODEL), 0.02),
        'w_router': nrm(13, (DEPTH, D_MODEL, N_EXPERTS), D_MODEL ** -0.5),
        'b_router': nrm(14, (DEPTH, N_EXPERTS), 0.01),
        'w_gate': nrm(15, (DEPTH, N_EXPERTS, D_MODEL, EXPERT_DFF), D_MODEL ** -0.5),
        'b_gate': nrm(16, (DEPTH, N_EXPERTS, EXPERT_DFF), 0.02),
        'w_up': nrm(17, (DEPTH, N_EXPERTS, D_MODEL, EXPERT_DFF), D_MODEL ** -0.5),
        'b_up': nrm(18, (DEPTH, N_EXPERTS, EXPERT_DFF), 0.02),
        'w_down': nrm(19, (DEPTH, N_EXPERTS, EXPERT_DFF, D_MODEL), DEEPNORM_BETA * EXPERT_DFF ** -0.5),
        'b_down': nrm(20, (DEPTH, N_EXPERTS, D_MODEL), 0.02),
        'ln2_g': 1.0 + nrm(21, (DEPTH, D_MODEL), 0.02),
        'ln2_b': nrm(22, (DEPTH, D_MODEL), 0.02),
    }

def reference(x_prompt, x_sample, state_gla, cache_swa_k, cache_swa_v, w_in, w_gk_up, b_gk_up,
              gla_norm_g, swa_sinks, w_out, ln1_g, ln1_b, w_router, b_router, w_gate, b_gate,
              w_up, b_up, w_down, b_down, ln2_g, ln2_b):
    pos_prompt = jnp.arange(x_prompt.shape[1])
    pos_sample = PAST_LEN + jnp.arange(x_sample.shape[1])
    s0_prompt = jnp.zeros((x_prompt.shape[0], GLA_HEADS, GLA_DK, GLA_DV), jnp.float32)
    xp, xs = x_prompt, x_sample
    gla_p, gla_s, kp_l, vp_l, ks_l, vs_l = [], [], [], [], [], []
    for l in range(DEPTH):
        weights = (w_in[l], w_gk_up[l], b_gk_up[l], gla_norm_g[l], swa_sinks[l], w_out[l],
                   ln1_g[l], ln1_b[l], w_router[l], b_router[l], w_gate[l], b_gate[l],
                   w_up[l], b_up[l], w_down[l], b_down[l], ln2_g[l], ln2_b[l])
        xp, sp, kp, vp = decoder_layer(xp, pos_prompt, s0_prompt, None, None, *weights)
        xs, ss, ksm, vsm = decoder_layer(xs, pos_sample, state_gla[l], cache_swa_k[l],
                                         cache_swa_v[l], *weights)
        gla_p.append(sp); gla_s.append(ss)
        kp_l.append(kp); vp_l.append(vp); ks_l.append(ksm); vs_l.append(vsm)
    state_gla_prompt = jnp.stack(gla_p)
    state_gla_sample = jnp.stack(gla_s)
    swa_k_prompt = jnp.stack(kp_l)
    swa_v_prompt = jnp.stack(vp_l)
    swa_k_sample = jnp.stack(ks_l)
    swa_v_sample = jnp.stack(vs_l)
    return (xp, xs, state_gla_prompt, state_gla_sample, swa_k_prompt, swa_v_prompt, swa_k_sample, swa_v_sample)


_drawn_inputs = setup_inputs


def setup_inputs(seed=0):
    import zlib

    import numpy as np

    out = dict(_drawn_inputs(seed))
    spreads = {}
    factors = {'gla_norm_g': 4.336,
     'swa_sinks': 5.437,
     'b_gate': 8.0,
     'b_up': 8.0,
     'b_down': 6.424,
     'ln2_g': 7.55,
     'ln2_b': 7.768,
     'b_router': 3.302}
    for name, (base, spread) in spreads.items():
        noise = np.random.default_rng([zlib.crc32(name.encode()), seed]).standard_normal(out[name].shape)
        drawn = base * np.exp(spread * noise) if base else spread * noise
        out[name] = __import__('jax').numpy.asarray(drawn.astype(out[name].dtype))
    for name, factor in factors.items():
        out[name] = (out[name] * factor).astype(out[name].dtype)
    return out
```

```python
from contextlib import ExitStack

import concourse.bass as bass
from concourse import mybir

F32 = mybir.dt.float32
F32R = mybir.dt.float32r
BF16 = mybir.dt.bfloat16
I32 = mybir.dt.int32
U32 = mybir.dt.uint32
ALU = mybir.AluOpType
ACT = mybir.ActivationFunctionType
AX = mybir.AxisListType.X

P = 128
D = 1024
KD = D // P
HALF = 512
SEQ = 512
NSEQ, DEC = 8, 4
NS = NSEQ * DEC
T = SEQ + NS
PT = SEQ // P
NT = PT + 1
GH, GDK, GDV = 4, 64, 128
AH, KVH, HD = 8, 2, 64
W = 128
NKEY = W + NS
ROT = 8
NE, TOPK = 32, 4
LIMIT, STEEP = 7.0, 1.702
EPS = 1e-5
ALPHA = 2.0 ** 0.25
NEG = -1.0e30
LEVELS = (64, 32, 16, 8, 4, 2, 1)
QK, GV, OG, LR, QS, KV, D_IN = 0, 512, 1024, 1536, 1552, 2064, 2320
MAXEXTRA = T * TOPK // P
YROWS = (NE + MAXEXTRA) * P

KEEP = dict(ident=P, iota=P, tokv=NT * 2, jcol=MAXEXTRA)
EARLY = dict(cum=P, rest=P, cum_s=NS, rest_s=NS, before=P, ones=P, upto32=2 * NE, cos=NT * ROT, sin=NT * ROT,
             win=2 * W, win_s=2 * NKEY, half=2, sel=2 * AH * NS, level=7 * 64, level_s=2 * 16,
             colseq=NSEQ * NS, rowseq=NSEQ, iota32=NE, eblock=NE, thr=4)

ORDER = ([f"x{i}" for i in range(NT)]
         + [f"proj{g}_{u}" for g in range(3) for u in range(3)] + ["lrT"]
         + [f"proj3_{u}" for u in range(3)] + ["z0", "z1"] + [f"proj4_{u}" for u in range(3)]
         + ["kT", "cacheT", "qT0", "qT1", "qT2", "cum0", "cum1", "rest0", "rest1",
            "qkT0", "qkT1", "qkT2"])
for _j in range(10):
    ORDER += [f"s{_j}"] * (_j < 8) + [f"level{_j}"] * (_j < 7) + [f"level_s{_j - 5}"] * (_j in (5, 6))
    ORDER += [f"pT{_j - 1}"] * (1 <= _j < 9) + [f"o{_j - 2}"] * (_j >= 2)
ORDER += ["ss", "spT", "so", "sel"]
ORDER += [f"ds{i}" for i in range(PT)] + [f"go{i}" for i in range(NT)] + ["sds0", "sds1"]
ORDER += [f"mixT{i}" for i in range(NT)] + [f"out{g}_{u}" for g in range(2) for u in range(3)]
for _i in range(NT + 1):
    ORDER += [f"x1T{_i}"] * (_i < NT) + [f"logit{_i - 1}"] * (_i > 0)
ORDER += ["pos", "xoff"]
USE = {name: n for n, name in enumerate(ORDER)}

SCORES = [(i, g) for i in range(PT) for g in range(KVH)]
GROUPS = [(None, 272), (QS, 512), (QK, 512), (GV, 512), (OG, 512)]
R1, S1 = 8, 4
NIN = 20
R2, S2 = 16, 8
PER = 3 * KD
EARLY_SPLIT = 4
YB = 3
AHEAD = 6


def rows(i):
    return P if i < PT else NS


def offsets(items):
    at, out = 0, {}
    for name, n in items.items():
        out[name] = (at, n)
        at += n
    return out, at


class Steps:

    def __init__(self, eng, own):
        self.eng, self.own, self.count, self.last = eng, own, {}, None

    def __call__(self, ins, sem=None, add=1):
        sem = self.own if sem is None else sem
        self.count[sem.name] = self.count.get(sem.name, 0) + add
        ins.then_inc(sem, 1)
        self.last = (sem, self.count[sem.name])

    def settle(self):
        self.eng.wait_ge(*self.last)


def build(nc, d):
    with ExitStack() as ctx:
        def sem(name):
            return ctx.enter_context(nc.semaphore(name))

        unit = [ctx.enter_context(nc.psum_tensor(f"unit{n}", [P, 1024], F32)) for n in range(4)]

        base = (nc.sbuf_base + 31) // 32 * 32
        here = [base]

        def sb(name, shape, dt=F32):
            size = 2 if dt == BF16 else 4
            for n in shape[1:]:
                size *= n
            t = nc.alloc_sbuf_tensor_at(name, shape, dt, offset=here[0])
            here[0] += (size + 31) // 32 * 32
            return t

        keep_at, nkeep = offsets(KEEP)
        early_at, nearly = offsets(EARLY)

        ck = sb("ck", [P, nkeep])
        posm = sb("posm", [P, NT, NE])
        gate4 = sb("gate4", [P, NT, TOPK])
        dest = sb("dest", [P, NT, TOPK], I32)
        shift = sb("shift", [P, MAXEXTRA])
        itab = sb("itab", [P, MAXEXTRA + 1], I32)
        eident = sb("eident", [64, NE])
        tokb = sb("tokb", [P, NT, 2], BF16)
        bias = sb("bias", [64, 3, D], F32R)
        raw_a = sb("raw_a", [P, R1, D])
        split_at = here[0]
        hi_a = sb("hi_a", [P, S1, D], F32R)
        lo_a = sb("lo_a", [P, S1, D], F32R)
        phase_at = here[0]

        ce = sb("ce", [P, nearly])
        params_at = here[0]
        lr = sb("lr", [P, NT, 16])
        lrT = sb("lrT_sb", [17, T])
        wgk = sb("wgk", [17, 256])
        negsink = sb("negsink", [P, AH])
        sink = sb("sink", [P, AH])
        sinkrow = sb("sinkrow", [P, 2])
        gnorm = sb("gnorm", [P, GDV])
        qkdot = sb("qkdot", [P, 20])
        nm = sb("nm", [P, 2, 4])
        mx = sb("mx", [P, 2, 4])
        es = sb("es", [P, 2, 4])
        den = sb("den", [P, 2, 4])
        rr = sb("rr", [P, 8, 4])
        snm = sb("snm", [P, 2])
        sden = sb("sden", [P, 2])
        ses = sb("ses", [P, 2])
        srr = sb("srr", [P, 2])
        ms = sb("ms", [P, NT * GH])
        xbuf_at = here[0]
        xbuf = sb("xbuf", [P, 2, D])
        here[0] = xbuf_at
        sbuf = sb("sbuf", [P, 2, 4, 2 * W])
        qkv_at = here[0]
        qkv = sb("qkv", [P, NT, 768])
        qk_at = here[0]
        qk = sb("qk", [P, NT, 512])
        gv = sb("gv", [P, NT, 512])
        og_at = here[0]
        og = sb("og", [P, NT, 512])
        big_end = here[0]
        here[0] = qk_at
        braw = sb("braw", [64, 3, D])
        btmp = sb("btmp", [64, 3, D], F32R)
        assert here[0] <= big_end
        here[0] = qk_at
        res = sb("res", [P, NT, D])
        here[0] = qkv_at
        ln_g = sb("ln_g", [P, D])
        ln_b = sb("ln_b", [P, D])
        here[0] = og_at
        x1T = sb("x1T", [P, KD, P])
        wr = sb("wr", [P, KD, NE])
        br = sb("br", [P, NE])
        lg = sb("lg", [P, NE])
        top8 = sb("top8", [P, 8])
        idx8 = sb("idx8", [P, 8], U32)
        idxf = sb("idxf", [P, TOPK])
        ntop = sb("ntop", [P, 1])
        gsum = sb("gsum", [P, 1])
        stats = sb("stats", [P, NT, 2, 6])
        mv = sb("mv", [P, NT, 2])
        rstd = sb("rstd", [P, NT])
        onehot = sb("onehot", [P, NT, TOPK, NE])
        assert here[0] <= big_end
        here[0] = big_end
        xt_at = here[0]
        xth = sb("xth", [P, KD, T], F32R)
        xtl = sb("xtl", [P, KD, T], F32R)
        xt_end = here[0]
        here[0] = xt_at
        s0 = sb("s0", [P, NSEQ, 2, GDV])
        state = sb("state", [P, PT, 2, GDV])
        qTa = sb("qTa", [P, 4, T])
        kTa = sb("kTa", [P, T])
        kcT = sb("kcT", [P, NSEQ, W])
        cum = sb("cum", [P, 2, T])
        qz = sb("qz", [P, NSEQ, AH, DEC])
        assert here[0] <= xt_end
        here[0] = xt_end
        eb = sb("eb", [P, 2, T])
        az = sb("az", [P, NT, 256])
        er = sb("er", [P, NT, 256])
        cV = sb("cV", [P, NSEQ, P])
        here_cK = here[0]
        cK = sb("cK", [P, NSEQ, P])
        here[0] = here_cK
        pT = sb("pT", [P, 2, 2, 4, P])
        phase_end = here[0]
        here[0] = split_at
        attT = sb("attT", [P, 16, P])
        attS = sb("attS", [NS, 4, NS])
        E = sb("E", [P, 2, T])
        kE = sb("kE", [P, 2, T])
        qR = sb("qR", [P, 2, T // 2])
        qkT = sb("qkT", [P, 4, T])
        assert here[0] <= phase_at
        here[0] = xbuf_at
        ssb = sb("ssb", [P, 2, NKEY])
        spT = sb("spT_sb", [P, 2, P])
        spTn = sb("spTn", [NS, 2, P])
        sos = sb("sos", [P, 2, KVH, HD])
        qbm = sb("qbm", [P, 2, NSEQ, NS])
        assert here[0] <= qkv_at
        here[0] = xbuf_at
        sq = sb("sq", [P, 2, 512])
        here[0] = here_cK
        kdm = sb("kdm", [NS, NSEQ, 256])
        here[0] = xbuf_at
        posf = sb("posf", [P, NT, NE])
        msk = sb("msk", [P, NT, NE])
        dmat = sb("dmat", [P, NT, NE])
        dsel = sb("dsel", [P, NT, TOPK, NE])
        xb = sb("xb", [P, 8])
        xbb = sb("xbb", [NE, P])
        xo = sb("xo", [P, 2 * NE])
        rowb = sb("rowb", [P, NE])
        assert here[0] <= qkv_at
        here[0] = xt_end
        xle = sb("xle", [P, MAXEXTRA, NE])
        xlm = sb("xlm", [P, MAXEXTRA, NE])
        exf = sb("exf", [P, MAXEXTRA + 1])
        destf = sb("destf", [P, NT * TOPK])

        here[0] = phase_at
        hi_b = sb("hi_b", [P, S2 - S1, D], F32R)
        lo_b = sb("lo_b", [P, S2 - S1, D], F32R)
        xeh = sb("xeh", [P, 2, KD, P], F32R)
        xel = sb("xel", [P, 2, KD, P], F32R)
        heh = sb("heh", [P, KD, P], F32R)
        hel = sb("hel", [P, KD, P], F32R)
        xg = sb("xg", [P, D])
        assert here[0] <= xt_at
        here[0] = xt_at
        raw_b = sb("raw_b", [P, R2 - R1, D])
        gm = sb("gm", [P, D])
        sg = sb("sg", [P, D])
        hb = sb("hb", [P, D])
        ysb = sb("ysb", [P, D])
        pick = sb("pick", [P, NT, P], BF16)
        selr = sb("selr", [64, 2, P], F32R)
        idx = sb("idx", [P, 2], I32)
        xpos = sb("xpos", [P, NT])
        assert here[0] <= nc.sbuf_usable_end, here[0]
        here[0] = phase_at
        yk = sb("yk", [P, YB, TOPK, D])
        acc = raw_a[:, 0:NT]
        g2, b2 = raw_a[:, NT], raw_a[:, NT + 1]
        st2 = sb("st2", [P, NT, 2, 6])
        mv2 = sb("mv2", [P, NT, 2])
        rs2 = sb("rs2", [P, NT])
        nmean2 = sb("nmean2", [P, NT])
        here[0] = phase_at
        xeT = sb("xeT", [P, KD, P])
        heT = sb("heT", [P, KD, P])
        selx = sb("selx", [64, P], F32R)
        eidx = sb("eidx", [P, 1], I32)

        raw = [raw_a[:, s] for s in range(R1)] + [raw_b[:, s] for s in range(R2 - R1)]
        hi = [hi_a[:, s] for s in range(S1)] + [hi_b[:, s] for s in range(S2 - S1)]
        lo = [lo_a[:, s] for s in range(S1)] + [lo_b[:, s] for s in range(S2 - S1)]

        def k_(name):
            a, n = keep_at[name]
            return ck[:, a:a + n]

        def c_(name):
            a, n = early_at[name]
            return ce[:, a:a + n]

        ident, iota = k_("ident"), k_("iota")

        x1_dram = nc.dram_tensor("x1_rows", (T, D), F32, kind="Internal").ap()
        y_dram = nc.dram_tensor("y_rows", (YROWS, D), F32, kind="Internal").ap()

        full = [sem(f"unit_full{n}") for n in range(4)]
        freed = [sem(f"unit_freed{n}") for n in range(4)]

        def filled(name):
            return full[USE[name] % 4], USE[name] // 4 + 1

        def emptied(name):
            return freed[USE[name] % 4], USE[name] // 4 + 1

        def emptied_after(name):
            return freed[USE[name] % 4], USE[name] // 4 + 2

        def s_full(name):
            return full[USE[name] % 4]

        def s_freed(name):
            return freed[USE[name] % 4]

        def bank(name):
            return unit[USE[name] % 4]

        const_in, bias_in, kc_in, s0_in, par_in = (sem(n) for n in ("const_in", "bias_in", "kc_in", "s0_in", "par_in"))
        x_in = [sem(f"x_in{n}") for n in range(2)]
        raw1_in = [sem(f"raw1_in{n}") for n in range(R1)]
        res_in, ln_in, wr_in = sem("res_in"), sem("ln_in"), sem("wr_in")
        out_done, x1_out = sem("out_done"), sem("x1_out")
        dve, act_s = sem("dve_step"), sem("act_step")
        x_hi, x_lo, hi1, lo1, used1 = (sem(n) for n in ("x_hi", "x_lo", "hi1", "lo1", "used1"))
        bias_hi_done, bias_ready = sem("bias_hi_done"), sem("bias_ready")
        proj_part = sem("proj_part")
        proj_out = sem("proj_out")
        rope_done, lrT_ready, z_abs, z_log, gk_ready = (sem(n) for n in (
            "rope_done", "lrT_ready", "z_abs", "z_log", "gk_ready"))
        kT_ready, qT_ready, cache_T, cum_ready, eb_ready, er_ready, kd_ready = (sem(n) for n in (
            "kT_ready", "qT_ready", "cache_T", "cum_ready", "eb_ready", "er_ready", "kd_ready"))
        sig_ready, gated, arg_ready, e_ready, ops_ready = (sem(n) for n in (
            "sig_ready", "gated", "arg_ready", "e_ready", "ops_ready"))
        nm_ready, p_ready, pT_ready, att_ready, qb_ready = (sem(n) for n in (
            "nm_ready", "p_ready", "pT_ready", "att_ready", "qb_ready"))
        snm_ready, sp_ready, spT_ready, sos_ready, selo = (sem(n) for n in (
            "snm_ready", "sp_ready", "spT_ready", "sos_ready", "selo"))
        state_ready, sstate_ready, go_out, ms_ready, rms_ready, mix_ready = (sem(n) for n in (
            "state_ready", "sstate_ready", "go_out", "ms_ready", "rms_ready", "mix_ready"))
        var_ready, std_ready, x1_ready, x1T_ready, ntop_ready, g_exp, mask_ready, xb_ready = (
            sem(n) for n in ("var_ready", "std_ready", "x1_ready", "x1T_ready", "ntop_ready",
                             "g_exp", "mask_ready", "xb_ready"))
        routed = sem("routed")
        w_in2 = [sem(f"w_in{n}") for n in range(R2)]
        split_hi, split_lo, slot_used = sem("split_hi"), sem("split_lo"), sem("slot_used")
        picked, tok_done, idx_ready, x_rows, xT_done, xe_hi, xe_lo = (sem(n) for n in (
            "picked", "tok_done", "idx_ready", "x_rows", "xT_done", "xe_hi", "xe_lo"))
        sel_ready, gate_read, sig2, h_ready, qz_ready, ones_ready = (sem(n) for n in (
            "sel_ready", "gate_read", "sig2", "h_ready", "qz_ready", "ones_ready"))
        h_part, hT_done, he_hi, he_lo, y_ready, y_stored = (sem(n) for n in (
            "h_part", "hT_done", "he_hi", "he_lo", "y_ready", "y_stored"))
        v_w, v_used, v_pick, v_tok, v_idx, v_rows, v_T, v_xT, v_g, v_gm, v_sg, v_u, v_h, v_hT, v_heT, v_y, v_ysb, \
            v_store, v_sel = (sem("extra_" + n) for n in (
                "weights", "used", "pick", "tok", "idx", "rows", "T", "xT", "gate", "gm", "sg", "up", "h", "hT",
                "heT", "y", "ysb", "store", "sel"))
        yk_in = [sem(f"yk_in{n}") for n in range(YB)]
        x1b_in, final_out, res_ready = sem("x1b_in"), sem("final_out"), sem("res_ready")
        nmean_ready, normed, scaled = sem("nmean_ready"), sem("normed"), sem("scaled")
        g2_in, acc_read, var2, std2, fin = (sem(n) for n in (
            "g2_in", "acc_read", "var2", "std2", "fin"))
        v_hm, kdm_ready = sem("extra_half"), sem("kdm_ready")
        y_free = sem("y_free")
        ended, turn_over = sem("ended"), sem("turn_over")

        block = ctx.enter_context(nc.Block())

        def w1_part(n):
            if n < NIN:
                g, s = divmod(n, 4)
                col, w = GROUPS[g]
                return d["w_in"][0, s * 256:(s + 1) * 256], col, w
            g, s = divmod(n - NIN, 4)
            return d["w_out"][0, s * 256:(s + 1) * 256], g * HALF, HALF

        OUTS = 3 + 2 + 2 * NSEQ + 2

        @block.sync
        def _(sp):
            sp.dma_start(ck[:], d["keep"][:, :]).then_inc(const_in, 16)
            for i in range(2):
                sp.dma_start(xbuf[:rows(i), i], d["x_prompt"][0, i * P:(i + 1) * P]).then_inc(x_in[i], 16)
            for n in range(NIN + 8):
                if n >= R1:
                    sp.wait_ge(lo1, n - R1 + 1)
                src, col, w = w1_part(n)
                dst = raw[n % R1][:, 0:2 * w].rearrange("p (k f) -> p k f", k=2)
                if col is None:
                    sp.dma_start(dst[:, :, 0:16], src[:, LR:LR + 16].rearrange("(k p) f -> p k f", p=P))\
                        .then_inc(raw1_in[n % R1], 16)
                    sp.dma_start(dst[:, :, 16:272], src[:, KV:D_IN].rearrange("(k p) f -> p k f", p=P))\
                        .then_inc(raw1_in[n % R1], 16)
                else:
                    sp.dma_start(dst, src[:, col:col + w].rearrange("(k p) f -> p k f", p=P))\
                        .then_inc(raw1_in[n % R1], 16)
                if n == 1:
                    sp.dma_start(ce[:], d["early"][:, :]).then_inc(const_in, 16)
                if 1 <= n <= 3:
                    i = n + 1
                    sp.wait_ge(*filled(f"x{i - 2}"))
                    src = d["x_prompt"][0, i * P:(i + 1) * P] if i < PT else d["x_sample"].rearrange("n t d -> (n t) d")
                    sp.dma_start(xbuf[:rows(i), i % 2], src).then_inc(x_in[i % 2], 16)
            sp.wait_ge(mix_ready, 1)
            sp.wait_ge(*filled("sds1"))
            sp.dma_start(res[:, 0:PT], d["x_prompt"][0].rearrange("(i p) d -> p i d", p=P)).then_inc(res_in, 16)
            sp.dma_start(res[:NS, PT], d["x_sample"].rearrange("n t d -> (n t) d")).then_inc(res_in, 16)
            sp.wait_ge(*filled(f"mixT{PT}"))
            sp.dma_start(ln_g[:], d["ln1_g"].partition_broadcast(P)).then_inc(ln_in, 16)
            sp.dma_start(ln_b[:], d["ln1_b"].partition_broadcast(P)).then_inc(ln_in, 16)
            sp.dma_start(wr[:], d["w_router"][0].rearrange("(k p) e -> p k e", p=P)).then_inc(wr_in, 16)
            sp.dma_start(br[:], d["b_router"].partition_broadcast(P)).then_inc(wr_in, 16)

            def weights(e, names, m0, it=None):
                m = m0
                for name in names:
                    src = d[name]
                    for k in range(KD):
                        turns = m if it is None else it * (2 * PER) + m
                        sp.wait_ge(split_lo, turns + 1)
                        if it is None:
                            w = src[0, e, k * P:(k + 1) * P]
                        else:
                            w = src[0, bass.ds(e, 1), k * P:(k + 1) * P].rearrange("a p f -> (a p) f")
                        sp.dma_start(raw[m % R2], w).then_inc(w_in2[m % R2], 16)
                        m += 1

            sp.wait_ge(lo1, NIN + 8)
            weights(0, ["w_gate"], 0)
            sp.wait_ge(used1, NIN + 8)
            with sp.Fori(0, NE // 2 - 1) as it:
                for par in range(2):
                    e = it * 2 + par
                    weights(e, ["w_up"], KD + PER * par, it)
                    weights(e + 1, ["w_gate"], 2 * KD + PER * par, it)
                    weights(e, ["w_down"], 3 * KD + PER * par, it)
            e = NE - 2
            weights(e, ["w_up"], KD + PER * e)
            weights(e + 1, ["w_gate"], 2 * KD + PER * e)
            weights(e, ["w_down"], 3 * KD + PER * e)
            weights(e + 1, ["w_up", "w_down"], KD + PER * (e + 1))

            sp.wait_ge(split_lo, KD + PER * (NE - 1) + KD + R2)
            sp.dma_start(acc[:, 0:PT], x1_dram[0:SEQ].rearrange("(i p) d -> p i d", p=P)).then_inc(x1b_in, 16)
            sp.dma_start(acc[:NS, PT], x1_dram[SEQ:T]).then_inc(x1b_in, 16)
            sp.dma_start(g2, d["ln2_g"].partition_broadcast(P)).then_inc(g2_in, 16)
            sp.dma_start(b2, d["ln2_b"].partition_broadcast(P)).then_inc(g2_in, 16)

            sp.wait_ge(routed, 1)
            n_extra = sp.value_load(itab[0:1, MAXEXTRA:MAXEXTRA + 1], min_val=0, max_val=MAXEXTRA)
            with sp.If(n_extra > 0):
                with sp.Fori(0, MAXEXTRA) as j:
                    with sp.If(j < n_extra):
                        ex = sp.value_load(itab[0:1, bass.ds(j, 1)], min_val=0, max_val=NE - 1)
                        for a, name in enumerate(("w_gate", "w_up", "w_down")):
                            sp.wait_ge(v_used, j * 3 + a + 1)
                            sp.dma_start(raw_b[:], d[name][0, bass.ds(ex, 1)].rearrange("a (k p) f -> p (a k) f", p=P))\
                                .then_inc(v_w, 16)

            for i in range(NT):
                sp.wait_ge(fin, i + 1)
                dst = d["y_p"][0, i * P:(i + 1) * P] if i < PT else d["y_s"].rearrange("n t d -> (n t) d")
                sp.dma_start(dst, acc[:rows(i), i]).then_inc(final_out, 16)
            sp.wait_ge(final_out, 16 * NT)
            sp.wait_ge(out_done, 16 * OUTS)

        @block.gpsimd
        def _(pool):
            pool.wait_ge(x_in[0], 32)
            pool.dma_start(braw[0:NE, 0], d["b_gate"][0]).then_inc(bias_in, 16)
            pool.dma_start(braw[NE:2 * NE, 0], d["b_gate"][0]).then_inc(bias_in, 16)
            pool.dma_start(braw[0:NE, 1], d["b_up"][0]).then_inc(bias_in, 16)
            pool.dma_start(braw[NE:2 * NE, 1], d["b_up"][0]).then_inc(bias_in, 16)
            pool.dma_start(braw[0:NE, 2], d["b_down"][0]).then_inc(bias_in, 16)
            pool.dma_start(braw[NE:2 * NE, 2], d["b_down"][0]).then_inc(bias_in, 16)
            pool.dma_start(wgk[0:16], d["w_gk_up"][0]).then_inc(par_in, 16)
            pool.dma_start(wgk[16:17], d["b_gk_up"]).then_inc(par_in, 16)
            pool.dma_start(sink[:], d["swa_sinks"].partition_broadcast(P)).then_inc(par_in, 16)
            pool.dma_start(sinkrow[:, 0:1], d["sinkrow"][:, :]).then_inc(par_in, 16)
            pool.dma_start(gnorm[:], d["gla_norm_g"].partition_broadcast(P)).then_inc(par_in, 16)
            pool.dma_start(eident[:], d["eident"][:, :]).then_inc(par_in, 16)
            pool.dma_start(cK[:], d["cache_k"][0].rearrange("n w k d -> w n (k d)")).then_inc(kc_in, 16)
            pool.dma_start(cV[:], d["cache_v"][0].rearrange("n w k d -> w n (k d)")).then_inc(kc_in, 16)
            pool.dma_start(d["ks"][0, :, 0:W - DEC], d["cache_k"][0, :, DEC:W]).then_inc(out_done, 16)
            pool.dma_start(d["vs"][0, :, 0:W - DEC], d["cache_v"][0, :, DEC:W]).then_inc(out_done, 16)
            pool.wait_ge(used1, 8)
            pool.dma_start(y_dram[NE * P:YROWS], d["w_gate"][0].rearrange("e k f -> (e k) f")[0:MAXEXTRA * P])\
                .then_inc(out_done, 16)
            pool.wait_ge(used1, NIN)
            pool.dma_start(s0[:], d["state_gla"][0].rearrange("n (a q) d e -> (q d) (n a) e", q=2)
                           .rearrange("p (n a) e -> p n a e", a=2)).then_inc(s0_in, 16)
            pool.wait_ge(rope_done, 1)
            for name, at in (("kp", 512), ("vp", 640)):
                pool.dma_start(d[name][0, 0].rearrange("w k d -> w (k d)"), qkv[:, PT - 1, at:at + 128])\
                    .then_inc(out_done, 16)
            for name, at in (("ks", 512), ("vs", 640)):
                for n in range(NSEQ):
                    pool.dma_start(d[name][0, n, W - DEC:W].rearrange("w k d -> w (k d)"),
                                   qkv[n * DEC:(n + 1) * DEC, PT, at:at + 128]).then_inc(out_done, 16)
            pool.wait_ge(state_ready, PT)
            pool.dma_start(d["st_p"][0, 0].rearrange("(a q) d e -> (q d) a e", q=2), state[:, PT - 1])\
                .then_inc(out_done, 16)
            pool.wait_ge(sstate_ready, 2)
            pool.dma_start(d["st_s"][0].rearrange("n (a q) d e -> (q d) (n a) e", q=2),
                           s0[:].rearrange("p n a e -> p (n a) e")).then_inc(out_done, 16)

            def gather(col):
                pool.indirect_dma_start(xg[:], None, x1_dram, bass.IndirectOffsetOnAxis(ap=idx[:, col:col + 1], axis=0))\
                    .then_inc(x_rows, 16)

            pool.wait_ge(out_done, 16 * OUTS)
            for i in range(NT):
                pool.wait_ge(x1_ready, i + 1)
                pool.dma_start(x1_dram[i * P:i * P + rows(i)], res[:rows(i), i]).then_inc(x1_out, 16)
            pool.wait_ge(x1_out, 16 * NT)
            pool.wait_ge(idx_ready, 1)
            gather(0)
            pool.wait_ge(idx_ready, 2)
            pool.wait_ge(xT_done, 1)
            pool.wait_ge(x_rows, 16)
            gather(1)

            def pool_step(e, par, n=None):
                n = e if n is None else n
                if not isinstance(e, int) or e < NE - 2:
                    pool.wait_ge(idx_ready, n + 3)
                    pool.wait_ge(xT_done, n + 2)
                    pool.wait_ge(x_rows, 16 * (n + 2))
                    pool.sem_inc(turn_over, 1)
                    gather(par)
                pool.wait_ge(y_ready, n + 2)
                dst = y_dram[e * P:(e + 1) * P] if isinstance(e, int) else y_dram[bass.ds(n * P, P)]
                pool.dma_start(dst, ysb[:]).then_inc(y_stored, 16)
                pool.wait_ge(y_stored, n * 16 + 16)
                pool.sem_inc(y_free, 1)

            pool.sem_inc(y_free, 1)
            with pool.Fori(0, NE // 2 - 1) as it:
                for par in range(2):
                    pool_step(it * 2 + par, par)
            for e in (NE - 2, NE - 1):
                pool_step(e, e % 2)

            n_extra = pool.value_load(itab[0:1, MAXEXTRA:MAXEXTRA + 1], min_val=0, max_val=MAXEXTRA)
            pool.wait_ge(y_stored, 16 * NE)
            pool.wait_ge(ended, 1)
            with pool.If(n_extra > 0):
                with pool.Fori(0, MAXEXTRA) as j:
                    with pool.If(j < n_extra):
                        pool.wait_ge(v_idx, j + 1)
                        pool.sem_inc(turn_over, 1)
                        pool.indirect_dma_start(xg[:], None, x1_dram, bass.IndirectOffsetOnAxis(ap=eidx[:, 0:1], axis=0))\
                            .then_inc(v_rows, 16)
                        pool.wait_ge(v_ysb, j + 1)
                        pool.dma_start(y_dram[bass.ds((j + NE) * P, P)], ysb[:]).then_inc(v_store, 16)
                        pool.wait_ge(v_store, (j + 1) * 16)
                        pool.sem_inc(turn_over, 1)
            pool.wait_ge(ended, 4)
            def outputs_of(i):
                if i >= YB:
                    pool.wait_ge(acc_read, i - YB + 1)
                for k in range(TOPK):
                    pool.indirect_dma_start(yk[:rows(i), i % YB, k], None, y_dram,
                                            bass.IndirectOffsetOnAxis(ap=dest[:rows(i), i, k:k + 1], axis=0))\
                        .then_inc(yk_in[i % YB], 16)

            def weigh(i):
                r, x_ = rows(i), acc[:rows(i), i]
                pool.wait_ge(normed, i + 1)
                pool.tensor_tensor(x_, x_, g2[:r], ALU.mult).then_inc(scaled, 1)
                pool.wait_ge(scaled, i + 1)
                pool.tensor_tensor(x_, x_, b2[:r], ALU.add).then_inc(fin, 1)

            for i in range(YB):
                outputs_of(i)
            pool.wait_ge(g2_in, 32)
            for i in range(NT):
                if i + YB < NT:
                    outputs_of(i + YB)
                weigh(i)

        @block.tensor
        def _(pe):
            mm, tr = nc.tensor.matmul, nc.tensor.transpose

            pe.sem_inc(slot_used, S2)

            def transposes(name, src, i):
                pe.wait_ge(*emptied(name))
                r = rows(i)
                for k in range(KD):
                    ins = tr(bank(name)[:, k * r:(k + 1) * r], src(k), ident[:r, :r])
                ins.then_inc(s_full(name), 1)

            def three(out, xh, xl, wh, wl, start, stop):
                mm(out, xh, wh, start=start, stop=False)
                mm(out, xh, wl, start=False, stop=False)
                return mm(out, xl, wh, start=False, stop=stop)

            pe.wait_ge(const_in, 16)
            for i in range(NT):
                pe.wait_ge(x_in[i % 2], 16 * (i // 2 + 1))
                transposes(f"x{i}", lambda k, i=i: xbuf[:rows(i), i % 2, k * P:(k + 1) * P], i)

            def weights_product(n0, n1, name):
                for n in range(n0, n1):
                    w = w1_part(n)[2]
                    pe.wait_ge(lo1, n + 1)
                    order = ([(kk, i) for u in range(3) for kk in range(2) for i in range(2 * u, min(2 * u + 2, NT))]
                             if n == n0 else [(kk, i) for kk in range(2) for i in range(NT)])
                    for kk, i in order:
                        if n == n0 and kk == 0 and i % 2 == 0:
                            pe.wait_ge(*emptied(f"{name}_{i // 2}"))
                        k = 2 * (n - n0) + kk
                        H = hi[n % S1][:, kk * w:(kk + 1) * w]
                        L = lo[n % S1][:, kk * w:(kk + 1) * w]
                        r = rows(i)
                        out = bank(f"{name}_{i // 2}")[:r, i % 2 * HALF:i % 2 * HALF + w]
                        ins = three(out, xth[:, k, i * P:i * P + r], xtl[:, k, i * P:i * P + r], H, L,
                                    k == 0, k == KD - 1)
                        if k == KD - 1 and i in (1, 3, 4):
                            ins.then_inc(s_full(f"{name}_{i // 2}"), 1)
                    if n == n1 - 1:
                        pe.drain().then_inc(used1, 1)
                    else:
                        ins.then_inc(used1, 1)

            pe.wait_ge(x_lo, NT)
            for g in range(5):
                weights_product(4 * g, 4 * g + 4, f"proj{g}")
                if g == 2:
                    pe.wait_ge(proj_out, 1)
                    pe.wait_ge(*emptied("lrT"))
                    for i in range(NT):
                        ins = tr(bank("lrT")[0:16, i * P:i * P + rows(i)], lr[:rows(i), i], ident[:rows(i), :rows(i)])
                    ins.then_inc(s_full("lrT"), 1)
                if g == 3:
                    pe.wait_ge(lrT_ready, 1)
                    pe.wait_ge(par_in, 16 * 6)
                    pe.wait_ge(*emptied("z0"))
                    for i in range(PT):
                        ins = mm(bank("z0")[:, i * 256:(i + 1) * 256], lrT[:, i * P:(i + 1) * P], wgk[:], start=True, stop=True)
                    ins.then_inc(s_full("z0"), 1)
                    pe.wait_ge(*emptied("z1"))
                    mm(bank("z1")[:NS, 0:256], lrT[:, SEQ:T], wgk[:], start=True, stop=True).then_inc(s_full("z1"), 1)
            pe.wait_ge(proj_out, 5)

            pe.wait_ge(rope_done, 1)
            pe.wait_ge(*emptied("kT"))
            for i in range(NT):
                ins = tr(bank("kT")[:, i * P:i * P + rows(i)], qkv[:rows(i), i, 512:640], ident[:rows(i), :rows(i)])
            ins.then_inc(s_full("kT"), 1)
            pe.wait_ge(kc_in, 32)
            pe.wait_ge(*emptied("cacheT"))
            for n in range(NSEQ):
                ins = tr(bank("cacheT")[:, n * W:(n + 1) * W], cK[:, n], ident)
            ins.then_inc(s_full("cacheT"), 1)
            for i in range(NT):
                name = f"qT{i // 2}"
                if i % 2 == 0:
                    pe.wait_ge(*emptied(name))
                r = rows(i)
                q4 = qkv[:r, i, 0:512].rearrange("p (j c) -> p j c", j=4)
                for j in range(4):
                    at = i % 2 * HALF + j * r
                    ins = tr(bank(name)[:, at:at + r], q4[:, j], ident[:r, :r])
                if i in (1, 3, 4):
                    ins.then_inc(s_full(name), 1)

            pe.wait_ge(gk_ready, 2)
            pe.wait_ge(*emptied("cum0"))
            for a in range(2):
                for i in range(PT):
                    ins = mm(bank("cum0")[:, a * HALF + i * P:a * HALF + (i + 1) * P], az[:, i, a * P:(a + 1) * P],
                             c_("cum"), start=True, stop=True)
            ins.then_inc(s_full("cum0"), 1)
            pe.wait_ge(*emptied("cum1"))
            for a in range(2):
                ins = mm(bank("cum1")[:, a * HALF:a * HALF + NS], az[:NS, PT, a * P:(a + 1) * P], c_("cum_s")[:NS],
                         start=True, stop=True)
            ins.then_inc(s_full("cum1"), 1)
            pe.wait_ge(*emptied("rest0"))
            for i in range(PT):
                ins = mm(bank("rest0")[:, i * 256:(i + 1) * 256], c_("rest"), az[:, i], start=True, stop=True)
            ins.then_inc(s_full("rest0"), 1)
            pe.wait_ge(*emptied("rest1"))
            mm(bank("rest1")[:NS, 0:256], c_("rest_s")[:NS], az[:NS, PT], start=True, stop=True)\
                .then_inc(s_full("rest1"), 1)
            for i in range(NT):
                name = f"qkT{i // 2}"
                if i % 2 == 0:
                    pe.wait_ge(*emptied(name))
                r = rows(i)
                for c in range(4):
                    at = i % 2 * HALF + c * r
                    ins = tr(bank(name)[:, at:at + r], qk[:r, i, c * P:(c + 1) * P], ident[:r, :r])
                if i in (1, 3, 4):
                    ins.then_inc(s_full(name), 1)

            def scores(j):
                i, g = SCORES[j]
                name, q0, k0 = f"s{j}", (0 if i else W), max(i - 1, 0) * W
                pe.wait_ge(*emptied(name))
                if j == 0:
                    pe.wait_ge(kT_ready, 1)
                    pe.wait_ge(qT_ready, NT)
                for h in range(4):
                    ins = mm(bank(name)[:, h * 2 * W + q0:(h + 1) * 2 * W], qTa[64 * g:64 * g + 64, h, i * P:(i + 1) * P],
                             kTa[64 * g:64 * g + 64, k0:(i + 1) * W], start=True, stop=True)
                ins.then_inc(s_full(name), 1)

            def prob_T(j):
                i, g = SCORES[j]
                name = f"pT{j}"
                pe.wait_ge(*emptied(name))
                pe.wait_ge(p_ready, j + 1)
                for kt in (range(2) if i else (1,)):
                    for h in range(4):
                        ins = tr(bank(name)[:, kt * HALF + h * P:kt * HALF + (h + 1) * P],
                                 sbuf[:, j % 2, h, kt * W:(kt + 1) * W], ident)
                ins.then_inc(s_full(name), 1)

            def values(j):
                i, g = SCORES[j]
                name = f"o{j}"
                pe.wait_ge(*emptied(name))
                pe.wait_ge(pT_ready, j + 1)
                for h in range(4):
                    kts = range(2) if i else (1,)
                    for kt in kts:
                        ins = mm(bank(name)[:, h * HD:(h + 1) * HD], pT[:, j % 2, kt, h],
                                 qkv[:, i - 1 + kt, 640 + g * HD:640 + (g + 1) * HD], start=kt == kts[0], stop=kt == 1)
                ins.then_inc(s_full(name), 1)

            def level(j):
                name = f"level{j}"
                pe.wait_ge(*emptied(name))
                pe.wait_ge(ops_ready, j + 1)
                for q in range(2):
                    for a in range(2):
                        for i in range(PT):
                            at = q * HALF + (a * PT + i) * 64
                            ins = mm(bank(name)[:, at:at + 64], kE[64 * q:64 * q + 64, a, i * P:(i + 1) * P],
                                     qR[64 * q:64 * q + 64, a, i * 64:(i + 1) * 64], start=True, stop=True)
                ins.then_inc(s_full(name), 1)
                if LEVELS[j] < DEC:
                    name = f"level_s{j - 5}"
                    pe.wait_ge(*emptied(name))
                    for q in range(2):
                        for a in range(2):
                            at = q * HALF + a * 16
                            ins = mm(bank(name)[:NS, at:at + 16], kE[64 * q:64 * q + 64, a, SEQ:T],
                                     qR[64 * q:64 * q + 64, a, SEQ // 2:T // 2], start=True, stop=True)
                    ins.then_inc(s_full(name), 1)

            for j in range(10):
                if j < 8:
                    scores(j)
                if j < 7:
                    level(j)
                if 1 <= j < 9:
                    prob_T(j - 1)
                if j >= 2:
                    values(j - 2)

            pe.wait_ge(*emptied("ss"))
            pe.wait_ge(cache_T, 1)
            pe.wait_ge(qz_ready, 1)
            for n in range(NSEQ):
                nn, c = n % 4, n // 4
                for at, keys in ((0, kcT[:, n]), (W, kTa[:, SEQ:T])):
                    w = W if at == 0 else NS
                    ins = mm(bank("ss")[32 * nn:32 * nn + 32, c * HALF + at:c * HALF + at + w],
                             qz[:, n].rearrange("p h t -> p (h t)"), keys, start=True, stop=True)
            ins.then_inc(s_full("ss"), 1)
            pe.wait_ge(*emptied("spT"))
            pe.wait_ge(sp_ready, 1)
            for c in range(2):
                tr(bank("spT")[:, c * P:(c + 1) * P], ssb[:, c, 0:W], ident)
            for c in range(2):
                ins = tr(bank("spT")[:NS, HALF + c * P:HALF + (c + 1) * P], ssb[:, c, W:NKEY], ident)
            ins.then_inc(s_full("spT"), 1)
            pe.wait_ge(*emptied("so"))
            pe.wait_ge(spT_ready, 1)
            for n in range(NSEQ):
                nn, c = n % 4, n // 4
                out = bank("so")[32 * nn:32 * nn + 32, c * P:(c + 1) * P]
                mm(out, spT[:, c, 32 * nn:32 * nn + 32], cV[:, n], start=True, stop=False)
                ins = mm(out, spTn[:, c, 32 * nn:32 * nn + 32], qkv[:NS, PT, 640:768], start=False, stop=True)
            ins.then_inc(s_full("so"), 1)
            pe.wait_ge(*emptied("sel"))
            pe.wait_ge(sos_ready, 1)
            pick_h = c_("sel").rearrange("p (c h t) -> p c h t", c=2, h=AH)
            for h in range(AH):
                for c in range(2):
                    ins = mm(bank("sel")[:NS, h * HD:(h + 1) * HD], pick_h[:, c, h], sos[:, c, h // 4],
                             start=c == 0, stop=c == 1)
            ins.then_inc(s_full("sel"), 1)

            pe.wait_ge(kd_ready, 2)
            for i in range(PT):
                name = f"ds{i}"
                pe.wait_ge(*emptied(name))
                for h in range(GH):
                    a, q = divmod(h, 2)
                    ins = mm(bank(name)[64 * q:64 * q + 64, a * GDV:(a + 1) * GDV], er[:, i, h * 64:(h + 1) * 64],
                             gv[:, i, h * GDV:(h + 1) * GDV], start=True, stop=True)
                ins.then_inc(s_full(name), 1)
            pe.wait_ge(att_ready, 1)
            pe.wait_ge(qb_ready, 1)
            for i in range(PT):
                name = f"go{i}"
                pe.wait_ge(*emptied(name))
                if i:
                    pe.wait_ge(state_ready, i)
                for h in range(GH):
                    a, q = divmod(h, 2)
                    out = bank(name)[:, q * HALF + a * GDV:q * HALF + (a + 1) * GDV]
                    ins = mm(out, attT[:, q * 8 + a * PT + i], gv[:, i, h * GDV:(h + 1) * GDV], start=True, stop=i == 0)
                    if i:
                        ins = mm(out, qkT[64 * q:64 * q + 64, a, i * P:(i + 1) * P], state[64 * q:64 * q + 64, i - 1, a],
                                 start=False, stop=True)
                ins.then_inc(s_full(name), 1)
            name = f"go{PT}"
            pe.wait_ge(*emptied(name))
            pe.wait_ge(s0_in, 16)
            for h in range(GH):
                a, q = divmod(h, 2)
                out = bank(name)[:NS, q * HALF + a * GDV:q * HALF + (a + 1) * GDV]
                mm(out, attS[:, q * 2 + a], gv[:NS, PT, h * GDV:(h + 1) * GDV], start=True, stop=False)
                for n in range(NSEQ):
                    ins = mm(out, qbm[64 * q:64 * q + 64, a, n], s0[64 * q:64 * q + 64, n, a], start=False,
                             stop=n == NSEQ - 1)
            ins.then_inc(s_full(name), 1)
            pe.wait_ge(kdm_ready, 1)
            for half in range(2):
                name = f"sds{half}"
                pe.wait_ge(*emptied(name))
                for n in range(4 * half, 4 * half + 4):
                    for h in range(GH):
                        a, q = divmod(h, 2)
                        at = (n % 4) * 256 + a * GDV
                        ins = mm(bank(name)[64 * q:64 * q + 64, at:at + GDV], kdm[:, n, h * 64:(h + 1) * 64],
                                 gv[:NS, PT, h * GDV:(h + 1) * GDV], start=True, stop=True)
                ins.then_inc(s_full(name), 1)

            pe.wait_ge(mix_ready, 1)
            pe.wait_ge(selo, 1)
            for i in range(NT):
                def src(k, i=i):
                    return (og[:rows(i), i, k * P:(k + 1) * P] if k < 4
                            else qkv[:rows(i), i, (k - 4) * P:(k - 3) * P])
                transposes(f"mixT{i}", src, i)
            pe.wait_ge(x_lo, 2 * NT)
            for g in range(2):
                weights_product(NIN + 4 * g, NIN + 4 * g + 4, f"out{g}")

            def x1_transposes(i):
                pe.wait_ge(x1_ready, i + 1)
                transposes(f"x1T{i}", lambda k: res[:rows(i), i, k * P:(k + 1) * P], i)

            x1_transposes(0)
            for i in range(NT):
                if i + 1 < NT:
                    x1_transposes(i + 1)
                name, r = f"logit{i}", rows(i)
                pe.wait_ge(*emptied(name))
                pe.wait_ge(x1T_ready, i + 1)
                pe.wait_ge(wr_in, 32)
                for k in range(KD):
                    ins = mm(bank(name)[:r, 0:NE], x1T[:, k, :r], wr[:, k], start=k == 0, stop=k == KD - 1)
                ins.then_inc(s_full(name), 1)
            pe.wait_ge(*emptied("pos"))
            for i in range(NT):
                pe.wait_ge(mask_ready, i + 1)
                out = bank("pos")[:rows(i), i * NE:(i + 1) * NE]
                for b in range(i):
                    mm(out, c_("ones")[:, :rows(i)], msk[:, b], start=b == 0, stop=False)
                mm(out, c_("before")[:rows(i), :rows(i)], msk[:rows(i), i], start=i == 0, stop=True)
            for i in range(NT):
                ins = mm(bank("pos")[:NE, NT * NE:NT * NE + 1], msk[:rows(i), i], c_("ones")[:rows(i), 0:1],
                         start=i == 0, stop=i == NT - 1)
            ins.then_inc(s_full("pos"), 1)
            pe.wait_ge(*emptied("xoff"))
            pe.wait_ge(xb_ready, 1)
            mm(bank("xoff")[:, 0:2 * NE], xbb[:], c_("upto32")[:NE], start=True, stop=True)\
                .then_inc(s_full("xoff"), 1)

            pg, pu, pd, px = unit

            def rows_of(done_sem):
                for i in range(NT):
                    ins = mm(px[:, 0:2], pick[:, i], tokb[:, i], start=i == 0, stop=i == NT - 1)
                ins.then_inc(done_sem, 1)

            def x_T():
                for k in range(KD):
                    ins = tr(px[:, k * P:(k + 1) * P], xg[:, k * P:(k + 1) * P], ident)
                ins.then_inc(xT_done, 1)

            def product(out, lh, ll, which, sel, m0, ks, it):
                if ks[0] == 0:
                    for h in range(2):
                        mm(out[:, h * HALF:(h + 1) * HALF], sel, bias[:, which, h * HALF:(h + 1) * HALF],
                           start=True, stop=False)
                for k in ks:
                    m = m0 + k
                    turns = m if it is None else it * (2 * PER) + m
                    pe.wait_ge(split_lo, turns + 1 + R2)
                    for h in range(2):
                        cols = slice(h * HALF, (h + 1) * HALF)
                        ins = three(out[:, cols], lh[:, k], ll[:, k], hi[m % S2][:, cols], lo[m % S2][:, cols],
                                    False, k == KD - 1)
                    ins.then_inc(slot_used, 1)

            pe.wait_ge(*emptied_after("xoff"))
            pe.wait_ge(picked, 1)
            rows_of(tok_done)
            pe.wait_ge(x_rows, 16)
            pe.wait_ge(idx_ready, 1)
            x_T()
            pe.wait_ge(xe_lo, 1)
            pe.wait_ge(picked, 2)
            rows_of(tok_done)
            pe.wait_ge(sel_ready, 1)
            pe.wait_ge(xe_hi, 1)
            product(pg, xeh[:, 0], xel[:, 0], 0, selr[:, 0], 0, range(KD), None)

            def pe_step(e, par, it=None, m0=None):
                last = isinstance(e, int) and e == NE - 1
                no_more = isinstance(e, int) and e >= NE - 2
                if not last:
                    pe.wait_ge(x_rows, (e + 2) * 16)
                    pe.wait_ge(idx_ready, e + 2)
                    pe.wait_ge(he_lo, e + 1)
                    x_T()
                else:
                    pe.wait_ge(he_lo, e + 1)
                pe.wait_ge(h_ready, e + 1)
                product(pu, xeh[:, par], xel[:, par], 1, selr[:, par], m0, range(KD), it)
                if not last:
                    pe.wait_ge(xe_lo, e + 2)
                    if not no_more:
                        pe.wait_ge(picked, e + 3)
                        rows_of(tok_done)
                    pe.wait_ge(sel_ready, e + 2)
                    pe.wait_ge(gate_read, e + 2)
                    nxt = (pg, xeh[:, 1 - par], xel[:, 1 - par], 0, selr[:, 1 - par], m0 + KD)
                    product(*nxt, range(KD - 2), it)
                    if not no_more:
                        pe.wait_ge(idx_ready, e + 3)
                pe.wait_ge(h_ready, e + 2)
                for k in range(KD):
                    ins = tr(px[:, k * P:(k + 1) * P], hb[:, k * P:(k + 1) * P], ident)
                ins.then_inc(hT_done, 1)
                if not last:
                    product(*nxt, range(KD - 2, KD), it)
                pe.wait_ge(he_lo, e + 2)
                pe.wait_ge(y_ready, e + 1)
                product(pd, heh, hel, 2, selr[:, par], m0 + (KD if last else 2 * KD), range(KD), it)

            with pe.Fori(0, NE // 2 - 1) as it:
                for par in range(2):
                    pe_step(it * 2 + par, par, it, KD + PER * par)
            for e in (NE - 2, NE - 1):
                pe_step(e, e % 2, None, KD + PER * e)

            pe.wait_ge(y_ready, NE + 1)
            pe.drain().then_inc(ended, 1)
            pe.sem_inc(v_used, 1)
            n_extra = pe.value_load(itab[0:1, MAXEXTRA:MAXEXTRA + 1], min_val=0, max_val=MAXEXTRA)
            with pe.If(n_extra > 0):
                with pe.Fori(0, MAXEXTRA) as j:
                    with pe.If(j < n_extra):
                        pe.wait_ge(v_pick, j + 1)
                        rows_of(v_tok)
                        pe.wait_ge(v_rows, (j + 1) * 16)
                        for k in range(KD):
                            ins = tr(px[:, k * P:(k + 1) * P], xg[:, k * P:(k + 1) * P], ident)
                        ins.then_inc(v_T, 1)
                        pe.wait_ge(v_sel, j + 1)
                        for a, (out, lhs, ready, done) in enumerate(((pg, xeT, v_xT, v_g), (pu, xeT, v_xT, v_u),
                                                                     (pd, heT, v_heT, v_y))):
                            if a == 2:
                                pe.wait_ge(v_h, j + 1)
                                for k in range(KD):
                                    ins = tr(px[:, k * P:(k + 1) * P], hb[:, k * P:(k + 1) * P], ident)
                                ins.then_inc(v_hT, 1)
                            pe.wait_ge(ready, j + 1)
                            pe.wait_ge(v_w, (j * 3 + a + 1) * 16)
                            for h in range(2):
                                cols = slice(h * HALF, (h + 1) * HALF)
                                mm(out[:, cols], selx[:], bias[:, a, cols], start=True, stop=False)
                                for k in range(KD):
                                    ins = mm(out[:, cols], lhs[:, k], raw_b[:, k, cols], start=False, stop=k == KD - 1)
                            ins.then_inc(done, 1)
                            pe.drain().then_inc(v_used, 1)
                        pe.wait_ge(v_ysb, j + 1)
                        pe.sem_inc(turn_over, 1)
            pe.drain().then_inc(ended, 1)

        @block.scalar
        def _(act):
            st = Steps(act, act_s)
            copy = lambda out, src, scale=1.0: nc.scalar.activation(out, src, ACT.Copy, scale=scale)
            act.sem_inc(y_ready, 1)

            def unit_T(name, i):
                return bank(name)[:, 0:KD * rows(i)].rearrange("p (k r) -> p k r", k=KD)

            for i in range(NT):
                act.wait_ge(*filled(f"x{i}"))
                st(copy(xth[:, :, i * P:i * P + rows(i)], unit_T(f"x{i}", i)), x_hi)


            def slot_hi(n):
                w = 2 * w1_part(n)[2]
                turns = n // R1
                act.wait_ge(raw1_in[n % R1], 16 * (turns + 1 + (1 if n % R1 < 4 else 0)))
                if n >= S1:
                    act.wait_ge(used1, n - S1 + 1)
                st(copy(hi[n % S1][:, 0:w], raw[n % R1][:, 0:w]), hi1)

            def proj_copy(g):
                col, w = GROUPS[g]
                for u in range(3):
                    name = f"proj{g}_{u}"
                    r, tiles = (P, slice(2 * u, 2 * u + 2)) if u < 2 else (NS, slice(PT, NT))
                    src = bank(name)[:r, 0:(2 if u < 2 else 1) * HALF].rearrange("p (t f) -> p t f", f=HALF)
                    act.wait_ge(*filled(name))
                    if g == 0:
                        st(copy(lr[:r, tiles], src[:, :, 0:16]))
                        st(copy(qkv[:r, tiles, 512:768], src[:, :, 16:272]), proj_part)
                    elif g == 1:
                        q4 = qkv[:r, tiles, 0:512].rearrange("p t (j g d) -> p t g j d", j=4, g=2)
                        s4 = src.rearrange("p t (g j d) -> p t g j d", j=4, g=2)
                        st(copy(q4[:, :, 0], s4[:, :, 0]))
                        st(copy(q4[:, :, 1], s4[:, :, 1]), proj_part)
                    elif g == 2:
                        if u == 0:
                            act.wait_ge(bias_ready, 1)
                        st(copy(qk[:r, tiles, 0:256], src[:, :, 0:256], scale=GDK ** -0.5))
                        st(copy(qk[:r, tiles, 256:512], src[:, :, 256:512]), proj_part)
                    else:
                        st(copy((gv if g == 3 else og)[:r, tiles], src), proj_part)
                    act.wait_ge(proj_part, 3 * g + u + 1)
                    act.sem_inc(s_freed(name), 1)
                act.sem_inc(proj_out, 1)

            for n in range(NIN):
                slot_hi(n)
                if n == 5:
                    act.wait_ge(bias_in, 96)
                    flat = lambda t: t.rearrange("p m f -> p (m f)")
                    st(copy(flat(bias[0:NE]), flat(braw[0:NE])))
                    st(copy(flat(btmp[NE:2 * NE]), flat(braw[NE:2 * NE])), bias_hi_done)
                if n % 4 == 3 and n > 4:
                    proj_copy(n // 4 - 1)
                if n == 17:
                    act.wait_ge(*filled("lrT"))
                    act.wait_ge(ones_ready, 1)
                    st(copy(lrT[0:16], bank("lrT")[0:16, 0:T]))
                    st.settle()
                    act.sem_inc(lrT_ready, 1)
                    act.sem_inc(s_freed("lrT"), 1)
            for u, z in enumerate((az[:, 0:PT], az[:NS, PT:NT])):
                act.wait_ge(z_abs, u + 1)
                st(nc.scalar.activation(z, z, ACT.Exp))
                st.settle()
                st(nc.scalar.activation(z, z, ACT.Ln, bias=1.0), z_log)
            proj_copy(4)

            act.wait_ge(*filled("kT"))
            st(copy(kTa[:], bank("kT")[:, 0:T]), kT_ready)
            act.wait_ge(kT_ready, 1)
            act.sem_inc(s_freed("kT"), 1)
            act.wait_ge(*filled("cacheT"))
            st(copy(kcT[:].rearrange("p n w -> p (n w)"), bank("cacheT")[:]), cache_T)
            act.wait_ge(cache_T, 1)
            act.sem_inc(s_freed("cacheT"), 1)
            for i in range(NT):
                name, r = f"qT{i // 2}", rows(i)
                act.wait_ge(*filled(name))
                src = bank(name)[:, i % 2 * HALF:i % 2 * HALF + 4 * r].rearrange("p (j r) -> p j r", j=4)
                st(copy(qTa[:, :, i * P:i * P + r], src), qT_ready)
                if i in (1, 3, 4):
                    act.wait_ge(qT_ready, i + 1)
                    act.sem_inc(s_freed(name), 1)
            for u, (a, b) in enumerate(((0, SEQ), (SEQ, T))):
                name = f"cum{u}"
                src = bank(name)[:].rearrange("p (a t) -> p a t", a=2)[:, :, 0:b - a]
                act.wait_ge(*filled(name))
                st(copy(cum[:, :, a:b], src), cum_ready)
                st(nc.scalar.activation(eb[:, :, a:b], src, ACT.Exp), eb_ready)
                act.wait_ge(eb_ready, u + 1)
                act.sem_inc(s_freed(name), 1)
            act.wait_ge(qz_ready, 1)
            for u, (t, r) in enumerate(((slice(0, PT), P), (slice(PT, NT), NS))):
                name = f"rest{u}"
                act.wait_ge(*filled(name))
                w = 1024 if u == 0 else 256
                st(nc.scalar.activation(er[:r, t].rearrange("p t c -> p (t c)"), bank(name)[:r, 0:w], ACT.Exp),
                   er_ready)
                act.wait_ge(er_ready, u + 1)
                act.sem_inc(s_freed(name), 1)
            for u in range(3):
                if u == 2:
                    act.wait_ge(gated, 1)
                t, r = (slice(2 * u, 2 * u + 2), P) if u < 2 else (slice(PT, NT), NS)
                w = 1024 if u < 2 else 512
                st(nc.scalar.activation(xbuf[:r, u % 2, 0:w], og[:r, t].rearrange("p t c -> p (t c)"), ACT.Sigmoid),
                   sig_ready)

            def level_exp(j):
                wide = T if LEVELS[j] < DEC else SEQ
                act.wait_ge(arg_ready, j + 1)
                st(nc.scalar.activation(E[:, :, 0:wide], E[:, :, 0:wide], ACT.Exp), e_ready)

            def softmax_exp(j):
                i, g = SCORES[j]
                k0 = 0 if i else W
                act.wait_ge(nm_ready, j + 1)
                st(nc.scalar.activation(es[:, j % 2], es[:, j % 2], ACT.Exp))
                for h in range(4):
                    s = sbuf[:, j % 2, h, k0:2 * W]
                    st(nc.scalar.activation(s, s, ACT.Exp, bias=nm[:, j % 2, h:h + 1], accum_out=den[:, j % 2, h:h + 1]))
                st.settle()
                act.sem_inc(p_ready, 1)

            def prob_out(j):
                i, g = SCORES[j]
                name = f"pT{j}"
                act.wait_ge(*filled(name))
                if j >= 2:
                    act.wait_ge(*filled(f"o{j - 2}"))
                at = 0 if i else HALF
                src = bank(name)[:, at:1024]
                st(copy(pT[:, j % 2].rearrange("p k h q -> p (k h q)")[:, at:1024], src), pT_ready)
                act.wait_ge(pT_ready, j + 1)
                act.sem_inc(s_freed(name), 1)

            level_exp(0)
            for j in range(10):
                if j < 8:
                    softmax_exp(j)
                if 0 < j + 1 < 7:
                    level_exp(j + 1)
                if 1 <= j < 9:
                    prob_out(j - 1)

            act.wait_ge(snm_ready, 1)
            for c in range(2):
                st(nc.scalar.activation(ses[:, c:c + 1], snm[:, c:c + 1], ACT.Exp, bias=sinkrow[:, 0:1]))
                st(nc.scalar.activation(ssb[:, c], ssb[:, c], ACT.Exp, bias=snm[:, c:c + 1], accum_out=sden[:, c:c + 1]))
            st.settle()
            act.sem_inc(sp_ready, 1)
            act.wait_ge(*filled("spT"))
            st(copy(spT[:].rearrange("p c k -> p (c k)"), bank("spT")[:, 0:2 * P]))
            st(copy(spTn[:].rearrange("p c k -> p (c k)"), bank("spT")[:NS, HALF:HALF + 2 * P]))
            st.settle()
            act.sem_inc(spT_ready, 1)
            act.sem_inc(s_freed("spT"), 1)
            act.wait_ge(*filled("sel"))
            st(copy(qkv[:NS, PT, 0:512], bank("sel")[:NS, 0:512]), selo)
            act.wait_ge(selo, 1)
            act.sem_inc(s_freed("sel"), 1)
            act.wait_ge(kd_ready, 2)
            for i in range(NT):
                name = f"go{i}"
                act.wait_ge(*filled(name))
                st(copy(qk[:rows(i), i].rearrange("p (a q e) -> p q a e", a=2, q=2),
                        bank(name)[:rows(i)].rearrange("p (q x) -> p q x", q=2)[:, :, 0:2 * GDV]
                        .rearrange("p q (a e) -> p q a e", a=2)), go_out)
                act.wait_ge(go_out, i + 1)
                act.sem_inc(s_freed(name), 1)
                act.wait_ge(ms_ready, i + 1)
                m = ms[:rows(i), i * GH:(i + 1) * GH]
                st(nc.scalar.activation(m, m, ACT.Sqrt, scale=1.0 / GDV, bias=EPS), rms_ready)

            act.wait_ge(out_done, 16 * OUTS)
            for i in range(NT):
                name = f"mixT{i}"
                act.wait_ge(*filled(name))
                st(copy(xth[:, :, i * P:i * P + rows(i)], unit_T(name, i)), x_hi)
            for n in range(NIN, NIN + 8):
                slot_hi(n)
            for i in range(NT):
                act.wait_ge(var_ready, i + 1)
                st(nc.scalar.activation(rstd[:rows(i), i:i + 1], mv[:rows(i), i, 1:2], ACT.Sqrt, bias=EPS), std_ready)
            def hi_slot(m0, j, it=None):
                m = m0 + j
                turns = (m // R2 + 1) if it is None else it * (2 * PER // R2) + (m // R2 + 1)
                act.wait_ge(w_in2[m % R2], turns * 16)
                act.wait_ge(slot_used, (m if it is None else it * (2 * PER) + m) + 1)
                copy(hi[m % S2], raw[m % R2]).then_inc(split_hi, 1)

            act.wait_ge(used1, NIN + 8)
            for i in range(NT):
                if i < EARLY_SPLIT:
                    hi_slot(0, i)
                name = f"x1T{i}"
                act.wait_ge(*filled(name))
                if i:
                    act.wait_ge(*filled(f"logit{i - 1}"))
                st(copy(x1T[:, :, 0:rows(i)], unit_T(name, i)), x1T_ready)
                act.wait_ge(x1T_ready, i + 1)
                act.sem_inc(s_freed(name), 1)
                act.wait_ge(ntop_ready, i + 1)
                r = rows(i)
                st(nc.scalar.activation(gate4[:r, i], top8[:r, 0:TOPK], ACT.Exp, bias=ntop[:r]), g_exp)

            pg, pu, pd, px = unit

            def rows_hi(par):
                copy(xeh[:, par].rearrange("p k s -> p (k s)"), px[:]).then_inc(xe_hi, 1)

            def pick_expert(col, par):
                copy(selr[:, par], col.to_broadcast([64, P])).then_inc(sel_ready, 1)

            def sigmoid():
                nc.scalar.activation(sg[:], gm[:], ACT.Sigmoid, scale=STEEP).then_inc(sig2, 1)

            def next_rows(n, par):
                act.wait_ge(slot_used, (n - 1) * PER + KD + S2)
                pick_expert(eident[:, bass.ds(n, 1)], par)
                act.wait_ge(xT_done, n + 1)
                rows_hi(par)

            def y_out(e, m_end):
                act.wait_ge(slot_used, m_end + S2)
                act.wait_ge(y_free, e + 1)
                copy(ysb[:], pd[:]).then_inc(y_ready, 1)

            act.wait_ge(x1_out, 16 * NT)
            act.wait_ge(routed, 1)
            pick_expert(eident[:, 0:1], 0)
            act.wait_ge(xT_done, 1)
            rows_hi(0)
            for j in range(EARLY_SPLIT, KD + AHEAD):
                hi_slot(0, j)
            next_rows(1, 1)
            act.wait_ge(gate_read, 2)
            sigmoid()

            def act_step(e, par, it=None, m0=None):
                last = isinstance(e, int) and e == NE - 1
                for j in range(AHEAD, 2 * KD if last else PER + AHEAD):
                    hi_slot(m0, j, it)
                    if j == (12 if last else 18):
                        act.wait_ge(hT_done, e + 1)
                        copy(heh[:].rearrange("p k s -> p (k s)"), px[:]).then_inc(he_hi, 1)
                    if j == 22:
                        act.wait_ge(gate_read, e + 3)
                        sigmoid()
                y_out(e, e * PER + (3 * KD if last else 4 * KD))
                if not (isinstance(e, int) and e >= NE - 2):
                    next_rows(e + 2, par)

            with act.Fori(0, NE // 2 - 1) as it:
                for par in range(2):
                    act_step(it * 2 + par, par, it, KD + PER * par)
            for e in (NE - 2, NE - 1):
                act_step(e, e % 2, None, KD + PER * e)

            act.wait_ge(x1b_in, 32)
            for i in range(NT):
                copy(acc[:rows(i), i], acc[:rows(i), i], scale=ALPHA).then_inc(res_ready, 1)

            n_extra = act.value_load(itab[0:1, MAXEXTRA:MAXEXTRA + 1], min_val=0, max_val=MAXEXTRA)
            act.wait_ge(y_stored, 16 * NE)
            act.wait_ge(ended, 1)
            with act.If(n_extra > 0):
                with act.Fori(0, MAXEXTRA) as j:
                    with act.If(j < n_extra):
                        ex = act.value_load(itab[0:1, bass.ds(j, 1)], min_val=0, max_val=NE - 1)
                        copy(selx[:], eident[:, bass.ds(ex, 1)].to_broadcast([64, P])).then_inc(v_sel, 1)
                        act.wait_ge(v_T, j + 1)
                        copy(xeT[:].rearrange("p k s -> p (k s)"), px[:]).then_inc(v_xT, 1)
                        act.wait_ge(v_gm, j + 1)
                        nc.scalar.activation(sg[:], gm[:], ACT.Sigmoid, scale=STEEP).then_inc(v_sg, 1)
                        act.wait_ge(v_hT, j + 1)
                        copy(heT[:].rearrange("p k s -> p (k s)"), px[:]).then_inc(v_heT, 1)
                        act.wait_ge(v_y, j + 1)
                        copy(ysb[:], pd[:]).then_inc(v_ysb, 1)
                        act.wait_ge(v_store, (j + 1) * 16)
                        act.sem_inc(turn_over, 1)
            act.drain().then_inc(ended, 1)
            for i in range(NT):
                r = rows(i)
                act.wait_ge(var2, i + 1)
                nc.scalar.activation(rs2[:r, i:i + 1], mv2[:r, i, 1:2], ACT.Sqrt, bias=EPS).then_inc(std2, 1)
                act.wait_ge(nmean_ready, i + 1)
                nc.scalar.activation(acc[:r, i], acc[:r, i], ACT.Identity, scale=rs2[:r, i:i + 1],
                                     bias=nmean2[:r, i:i + 1]).then_inc(normed, 1)

        @block.vector
        def _(v):
            st = Steps(v, dve)
            tt, ts, stt, cp = nc.vector.tensor_tensor, nc.vector.tensor_scalar, nc.vector.scalar_tensor_tensor, \
                nc.vector.tensor_copy
            red = lambda out, src, op: nc.vector.tensor_reduce(out, src, AX, op)
            f = lambda t: t.bitcast(F32)

            for n in range(4):
                v.sem_inc(freed[n], 1)
            v.sem_inc(split_lo, R2)
            v.sem_inc(h_ready, 1)
            v.sem_inc(gate_read, 1)
            v.sem_inc(he_lo, 1)

            def unit_T(name, i):
                return bank(name)[:, 0:KD * rows(i)].rearrange("p (k r) -> p k r", k=KD)

            def part_lo(name, i, ready, n, done):
                c = slice(i * P, i * P + rows(i))
                v.wait_ge(ready, n)
                st(tt(xtl[:, :, c], unit_T(name, i), f(xth[:, :, c]), ALU.subtract), done)
                v.wait_ge(done, n)
                v.sem_inc(s_freed(name), 1)

            def slot_lo(n):
                w = 2 * w1_part(n)[2]
                v.wait_ge(hi1, n + 1)
                if n >= S1:
                    v.wait_ge(used1, n - S1 + 1)
                st(tt(lo[n % S1][:, 0:w], raw[n % R1][:, 0:w], f(hi[n % S1][:, 0:w]), ALU.subtract), lo1)

            for i in range(NT):
                part_lo(f"x{i}", i, x_hi, i + 1, x_lo)
            for n in range(NIN):
                slot_lo(n)
                if n == 6:
                    v.wait_ge(bias_hi_done, 1)
                    st(tt(bias[NE:2 * NE], braw[NE:2 * NE], f(btmp[NE:2 * NE]), ALU.subtract), bias_ready)
                if n == 8:
                    st(nc.vector.memset(lrT[:], 1.0), ones_ready)
                if n == 11:
                    v.wait_ge(proj_out, 2)
                    for r, t, nt in ((P, slice(0, PT), PT), (NS, slice(PT, NT), 1)):
                        heads = qkv[:r, t, 0:640].rearrange("p t (h e) -> p t h e", h=10)
                        x1, x2 = heads[:, :, :, 0:ROT], heads[:, :, :, ROT:2 * ROT]
                        cos, sin = (c_(name).rearrange("p (t f) -> p t f", t=NT)[:r, t].unsqueeze(2)
                                    .to_broadcast([r, nt, 10, ROT]) for name in ("cos", "sin"))
                        work = az[:].rearrange("p t c -> p (t c)").rearrange("p (w t h f) -> p w t h f", w=4, t=PT, h=10)
                        a, b, c, e = (work[:r, w, 0:nt] for w in range(4))
                        st(tt(a, x1, cos, ALU.mult))
                        st(tt(b, x2, sin, ALU.mult))
                        st(tt(c, x2, cos, ALU.mult))
                        st(tt(e, x1, sin, ALU.mult))
                        st.settle()
                        st(tt(x1, a, b, ALU.subtract))
                        st(tt(x2, c, e, ALU.add))
                        st.settle()
                    v.sem_inc(rope_done, 1)
            for u, (z, r, n) in enumerate(((az[:, 0:PT], P, PT), (az[:NS, PT:NT], NS, 1))):
                name = f"z{u}"
                src = bank(name)[:r, 0:n * 256].rearrange("p (t c) -> p t c", t=n)
                v.wait_ge(*filled(name))
                st(cp(z, src))
                st.settle()
                st(stt(z, z, -1.0, z, ALU.mult, ALU.min), z_abs)
            for u, (z, r, n) in enumerate(((az[:, 0:PT], P, PT), (az[:NS, PT:NT], NS, 1))):
                name = f"z{u}"
                flat_z = z.rearrange("p t c -> p (t c)")
                v.wait_ge(z_log, u + 1)
                st(stt(flat_z, bank(name)[:r, 0:n * 256], 0.0, flat_z, ALU.min, ALU.subtract), gk_ready)
                v.wait_ge(gk_ready, u + 1)
                v.sem_inc(s_freed(name), 1)
            v.wait_ge(par_in, 16 * 6)
            st(ts(negsink[:], sink[:], -1.0, None, ALU.mult))
            st(ts(sinkrow[:, 1:2], sinkrow[:, 0:1], -1.0, None, ALU.mult))
            st(cp(tokb[:].rearrange("p t c -> p (t c)"), k_("tokv")))
            v.wait_ge(proj_out, 3)
            for i in range(NT):
                r = rows(i)
                st(tt(er[:r, i], qk[:r, i, 0:256], qk[:r, i, 256:512], ALU.mult))
            st.settle()
            for i in range(NT):
                r = rows(i)
                src = er[:r, i].rearrange("p (a q e) -> p a q e", a=2, q=2)
                if i < PT:
                    out = qkdot[:, 0:16].rearrange("p (q a i) -> p i a q", q=2, a=2)[:, i]
                else:
                    out = qkdot[:r, 16:20].rearrange("p (q a) -> p a q", q=2)
                st(red(out, src, ALU.add))
            st.settle()
            v.wait_ge(proj_out, 5)
            st(tt(attT[:], ident.unsqueeze(1).to_broadcast([P, 16, P]),
                  qkdot[:, 0:16].unsqueeze(2).to_broadcast([P, 16, P]), ALU.mult))
            st(tt(attS[:], ident[:NS, :NS].unsqueeze(1).to_broadcast([NS, 4, NS]),
                  qkdot[:NS, 16:20].unsqueeze(2).to_broadcast([NS, 4, NS]), ALU.mult))
            st(nc.vector.memset(qz[:], 0.0))
            st.settle()
            v.sem_inc(qz_ready, 1)

            for i in range(NT):
                name, r = f"qkT{i // 2}", rows(i)
                v.wait_ge(*filled(name))
                src = bank(name)[:, i % 2 * HALF:i % 2 * HALF + 4 * r].rearrange("p (c r) -> p c r", c=4)
                st(cp(qkT[:, :, i * P:i * P + r], src))
                if i in (1, 3, 4):
                    st.settle()
                    v.sem_inc(s_freed(name), 1)
            st.settle()
            v.wait_ge(er_ready, 2)
            for r, t in ((P, slice(0, PT)), (NS, slice(PT, NT))):
                st(tt(er[:r, t], er[:r, t], qk[:r, t, 256:512], ALU.mult), kd_ready)

            def level_args(j):
                half = LEVELS[j]
                wide = T if half < DEC else SEQ
                b, e = (x[:, :, 0:wide].rearrange("p a (n r) -> p a n r", r=2 * half) for x in (cum, E))
                mid = b[:, :, :, half - 1:half].to_broadcast([P, 2, wide // (2 * half), half])
                st(tt(e[:, :, :, 0:half], mid, b[:, :, :, 0:half], ALU.subtract))
                st(tt(e[:, :, :, half:], b[:, :, :, half:], mid, ALU.subtract))
                st.settle()
                v.sem_inc(arg_ready, 1)

            def level_ops(j):
                half = LEVELS[j]
                wide = T if half < DEC else SEQ
                v.wait_ge(e_ready, j + 1)
                st(tt(kE[:, :, 0:wide], qkT[:, 2:4, 0:wide], E[:, :, 0:wide], ALU.mult))
                q, e = (x.rearrange("p a (n r) -> p a n r", r=2 * half)[:, :, :, half:]
                        for x in (qkT[:, 0:2, 0:wide], E[:, :, 0:wide]))
                st(tt(qR[:, :, 0:wide // 2].rearrange("p a (n r) -> p a n r", r=half), q, e, ALU.mult))
                st.settle()
                v.sem_inc(ops_ready, 1)

            def level_in(j):
                half, name = LEVELS[j], f"level{j}"
                v.wait_ge(*filled(name))
                mask = c_("level").bitcast(I32).rearrange("p (l n r) -> p l n r", l=7, r=half)[:, j].unsqueeze(1)\
                    .to_broadcast([P, 8, 64 // half, half])
                for q in range(2):
                    out = attT[:, 8 * q:8 * q + 8].rearrange("p b (n r) -> p b n r", r=2 * half)[:, :, :, half:]
                    src = bank(name)[:, q * HALF:(q + 1) * HALF].rearrange("p (b n r) -> p b n r", b=8, r=half)
                    st(nc.vector.copy_predicated(out, mask, src))
                st.settle()
                v.sem_inc(s_freed(name), 1)
                if half < DEC:
                    name = f"level_s{j - 5}"
                    v.wait_ge(*filled(name))
                    mask = c_("level_s").bitcast(I32).rearrange("p (l n r) -> p l n r", l=2, r=half)[:NS, j - 5]\
                        .unsqueeze(1).to_broadcast([NS, 2, 16 // half, half])
                    for q in range(2):
                        out = attS[:, 2 * q:2 * q + 2].rearrange("p b (n r) -> p b n r", r=2 * half)[:, :, :, half:]
                        src = bank(name)[:NS, q * HALF:q * HALF + 32].rearrange("p (b n r) -> p b n r", b=2, r=half)
                        st(nc.vector.copy_predicated(out, mask, src))
                    st.settle()
                    v.sem_inc(s_freed(name), 1)
                if j == 6:
                    v.sem_inc(att_ready, 1)

            def softmax_in(j):
                i, g = SCORES[j]
                name, k0 = f"s{j}", 0 if i else W
                v.wait_ge(*filled(name))
                if j >= 2:
                    v.wait_ge(*filled(f"pT{j - 2}"))
                s = sbuf[:, j % 2, :, k0:2 * W]
                src = bank(name)[:].rearrange("p (h k) -> p h k", h=4)[:, :, k0:2 * W]
                mask = c_("win")[:, k0:2 * W].unsqueeze(1).to_broadcast([P, 4, 2 * W - k0])
                st(stt(s, src, HD ** -0.5, mask, ALU.mult, ALU.add))
                st.settle()
                v.sem_inc(s_freed(name), 1)
                st(red(mx[:, j % 2], s, ALU.max))
                st.settle()
                st(stt(nm[:, j % 2], mx[:, j % 2], -1.0, negsink[:, 4 * g:4 * g + 4], ALU.mult, ALU.min))
                st.settle()
                st(tt(es[:, j % 2], nm[:, j % 2], sink[:, 4 * g:4 * g + 4], ALU.add))
                st.settle()
                v.sem_inc(nm_ready, 1)

            def softmax_sum(j):
                v.wait_ge(p_ready, j + 1)
                st(tt(den[:, j % 2], den[:, j % 2], es[:, j % 2], ALU.add))
                st.settle()
                st(nc.vector.reciprocal(rr[:, j], den[:, j % 2]))

            def attention_out(j):
                i, g = SCORES[j]
                name = f"o{j}"
                v.wait_ge(*filled(name))
                st.settle()
                st(tt(qkv[:, i, g * 256:(g + 1) * 256].rearrange("p (h e) -> p h e", h=4),
                      bank(name)[:, 0:256].rearrange("p (h e) -> p h e", h=4),
                      rr[:, j].unsqueeze(2).to_broadcast([P, 4, HD]), ALU.mult))
                st.settle()
                v.sem_inc(s_freed(name), 1)

            v.wait_ge(cum_ready, 2)
            level_args(0)
            for u in range(3):
                t, r, nt = (slice(2 * u, 2 * u + 2), P, 2) if u < 2 else (slice(PT, NT), NS, 1)
                v.wait_ge(sig_ready, u + 1)
                o_ = og[:r, t].rearrange("p t c -> p (t c)")
                st(tt(o_, o_, xbuf[:r, u % 2, 0:nt * 512], ALU.mult), gated)
            v.wait_ge(gated, 3)
            v.wait_ge(qT_ready, NT)
            for g in range(2):
                half = slice(64 * g, 64 * g + 64)
                st(cp(qz[half, :, 4 * g:4 * g + 4], qTa[half, :, SEQ:T].rearrange("p j (n t) -> p n j t", n=NSEQ)))
            st.settle()
            v.sem_inc(qz_ready, 1)
            for j in range(10):
                if j >= 7:
                    u = j - 7
                    t, r, nt = (slice(2 * u, 2 * u + 2), P, 2) if u < 2 else (slice(PT, NT), NS, 1)
                    o_ = og[:r, t].rearrange("p t (h e) -> p (t h) e", h=GH)
                    st(tt(o_, o_, gnorm[:r].unsqueeze(1).to_broadcast([r, nt * GH, GDV]), ALU.mult))
                if j < 7:
                    level_ops(j)
                if j + 1 < 7:
                    level_args(j + 1)
                if j < 8:
                    softmax_in(j)
                if j < 7:
                    level_in(j)
                if 1 <= j < 9:
                    softmax_sum(j - 1)
                if j >= 2:
                    attention_out(j - 2)

            name = "ss"
            v.wait_ge(*filled(name))
            st(stt(ssb[:], bank(name)[:].rearrange("p (c k) -> p c k", c=2)[:, :, 0:NKEY], HD ** -0.5,
                   c_("win_s").rearrange("p (c k) -> p c k", c=2), ALU.mult, ALU.add))
            st.settle()
            v.sem_inc(s_freed(name), 1)
            st(red(srr[:], ssb[:], ALU.max))
            st.settle()
            st(stt(snm[:], srr[:], -1.0, sinkrow[:, 1:2].to_broadcast([P, 2]), ALU.mult, ALU.min), snm_ready)
            v.wait_ge(sp_ready, 1)
            st(tt(sden[:], sden[:], ses[:], ALU.add))
            st.settle()
            st(nc.vector.reciprocal(srr[:], sden[:]))
            st.settle()
            v.wait_ge(*filled("so"))
            for c in range(2):
                st(stt(sos[:, c], bank("so")[:, c * P:(c + 1) * P].rearrange("p (g e) -> p g e", g=2), srr[:, c:c + 1],
                       c_("half").unsqueeze(2).to_broadcast([P, 2, HD]), ALU.mult, ALU.mult))
            st.settle()
            v.sem_inc(sos_ready, 1)
            v.sem_inc(s_freed("so"), 1)

            st(tt(qkT[:, 0:2], qkT[:, 0:2], eb[:], ALU.mult))
            v.wait_ge(eb_ready, 2)
            st.settle()
            st(tt(qbm[:], qkT[:, 0:2, SEQ:T].unsqueeze(2).to_broadcast([P, 2, NSEQ, NS]),
                  c_("colseq").rearrange("p (n t) -> p n t", n=NSEQ).unsqueeze(1).to_broadcast([P, 2, NSEQ, NS]),
                  ALU.mult))
            st.settle()
            v.sem_inc(qb_ready, 1)
            v.wait_ge(kd_ready, 2)
            st(tt(kdm[:], er[:NS, PT].unsqueeze(1).to_broadcast([NS, NSEQ, 256]),
                  c_("rowseq")[:NS].unsqueeze(2).to_broadcast([NS, NSEQ, 256]), ALU.mult), kdm_ready)
            for i in range(PT):
                name = f"ds{i}"
                v.wait_ge(*filled(name))
                src = bank(name)[:, 0:2 * GDV].rearrange("p (a e) -> p a e", a=2)
                if i == 0:
                    st(cp(state[:, 0], src))
                else:
                    for a in range(2):
                        st(stt(state[:, i, a], state[:, i - 1, a], eb[:, a, (i + 1) * P - 1:(i + 1) * P], src[:, a],
                               ALU.mult, ALU.add))
                st.settle()
                v.sem_inc(state_ready, 1)
                v.sem_inc(s_freed(name), 1)
            def norm_gate(i):
                r, m = rows(i), ms[:rows(i), i * GH:(i + 1) * GH]
                v.wait_ge(go_out, i + 1)
                st(tt(sq[:r, i % 2], qk[:r, i], qk[:r, i], ALU.mult))
                st.settle()
                st(red(m, sq[:r, i % 2].rearrange("p (h e) -> p h e", h=GH), ALU.add), ms_ready)
                v.wait_ge(rms_ready, i + 1)
                st(nc.vector.reciprocal(m, m))
                st.settle()
                o_ = qk[:r, i].rearrange("p (h e) -> p h e", h=GH)
                st(tt(o_, o_, m.unsqueeze(2).to_broadcast([r, GH, GDV]), ALU.mult))
                st.settle()
                st(tt(og[:r, i], og[:r, i], qk[:r, i], ALU.mult))
                st.settle()

            v.wait_ge(*filled("sel"))
            for i in range(PT):
                norm_gate(i)
            v.wait_ge(*filled(f"go{PT}"))
            decay = eb[:, :, SEQ:T].rearrange("p a (n t) -> p n a t", t=DEC)[:, :, :, DEC - 1:DEC]
            for half in range(2):
                name = f"sds{half}"
                s_ = s0[:, 4 * half:4 * half + 4]
                st(tt(s_, s_, decay[:, 4 * half:4 * half + 4].to_broadcast([P, 4, 2, GDV]), ALU.mult))
                st.settle()
                v.wait_ge(*filled(name))
                s_ = s_.rearrange("p n a e -> p (n a e)")
                st(tt(s_, s_, bank(name)[:], ALU.add))
                st.settle()
                v.sem_inc(sstate_ready, 1)
                v.sem_inc(s_freed(name), 1)

            norm_gate(PT)
            v.sem_inc(mix_ready, 1)

            for i in range(NT):
                part_lo(f"mixT{i}", i, x_hi, NT + i + 1, x_lo)
            for n in range(NIN, NIN + 8):
                slot_lo(n)

            def first_norm(i):
                r = rows(i)
                v.wait_ge(std_ready, i + 1)
                st(nc.vector.reciprocal(rstd[:r, i:i + 1], rstd[:r, i:i + 1]))
                x_ = res[:r, i]
                st(stt(x_, x_, mv[:r, i, 0:1], ln_g[:r], ALU.subtract, ALU.mult))
                st.settle()
                st(stt(x_, x_, rstd[:r, i:i + 1], ln_b[:r], ALU.mult, ALU.add), x1_ready)

            v.wait_ge(res_in, 32)
            v.wait_ge(ln_in, 32)
            for g in range(2):
                for u in range(3):
                    name = f"out{g}_{u}"
                    r, t, nt = (P, slice(2 * u, 2 * u + 2), 2) if u < 2 else (NS, slice(PT, NT), 1)
                    v.wait_ge(*filled(name))
                    x_ = res[:r, t, g * HALF:(g + 1) * HALF]
                    st(stt(x_, x_, ALPHA, bank(name)[:r, 0:nt * HALF].rearrange("p (t f) -> p t f", t=nt),
                           ALU.mult, ALU.add))
                    st.settle()
                    v.sem_inc(s_freed(name), 1)
                if g == 0:
                    for i in range(NT):
                        st(nc.vector.bn_stats(stats[:rows(i), i, 0], res[:rows(i), i, 0:HALF]))
            for i in range(NT):
                r = rows(i)
                st(nc.vector.bn_stats(stats[:r, i, 1], res[:r, i, HALF:D]))
                st.settle()
                st(nc.vector.bn_aggr(mv[:r, i], stats[:r, i].rearrange("p h s -> p (h s)")))
                st.settle()
                v.sem_inc(var_ready, 1)
                if i:
                    first_norm(i - 1)
            first_norm(NT - 1)

            def lo_slot(m0, j, it=None):
                m = m0 + j
                at = m if it is None else it * (2 * PER) + m
                v.wait_ge(split_hi, at + 1)
                v.wait_ge(slot_used, at + 1)
                tt(lo[m % S2], raw[m % R2], f(hi[m % S2]), ALU.subtract).then_inc(split_lo, 1)

            v.wait_ge(used1, NIN + 8)
            st(nc.vector.memset(onehot[:], 0.0))
            st(nc.vector.memset(msk[:], 0.0))
            st(nc.vector.memset(posf[:], 0.0))
            st.settle()
            v.wait_ge(wr_in, 32)
            for i in range(NT):
                name, r = f"logit{i}", rows(i)
                v.wait_ge(*filled(name))
                st(tt(lg[:r], bank(name)[:r, 0:NE], br[:r], ALU.add))
                st.settle()
                v.sem_inc(s_freed(name), 1)
                if i:
                    v.wait_ge(g_exp, i)
                st(nc.vector.max(top8[:r], lg[:r]))
                st.settle()
                st(nc.vector.max_index(idx8[:r], top8[:r], lg[:r]))
                st(ts(ntop[:r], top8[:r, 0:1], -1.0, None, ALU.mult))
                st.settle()
                v.sem_inc(ntop_ready, 1)
                st(cp(idxf[:r], idx8[:r, 0:TOPK]))
                st.settle()
                st(tt(onehot[:r, i], c_("iota32")[:r].unsqueeze(1).to_broadcast([r, TOPK, NE]),
                      idxf[:r].unsqueeze(2).to_broadcast([r, TOPK, NE]), ALU.is_equal))
                st.settle()
                st(red(msk[:r, i], onehot[:r, i].rearrange("p k e -> p e k"), ALU.add))
                st.settle()
                v.sem_inc(mask_ready, 1)
                if i < EARLY_SPLIT:
                    lo_slot(0, i)
                v.wait_ge(g_exp, i + 1)
                st(red(gsum[:r], gate4[:r, i], ALU.add))
                st.settle()
                st(nc.vector.reciprocal(gsum[:r], gsum[:r]))
                st.settle()
                st(ts(gate4[:r, i], gate4[:r, i], gsum[:r], None, ALU.mult))
            v.wait_ge(*filled("pos"))
            st(cp(posf[:, 0:PT].rearrange("p t e -> p (t e)"), bank("pos")[:, 0:PT * NE]))
            st(cp(posf[:NS, PT], bank("pos")[:NS, PT * NE:NT * NE]))
            st(tt(xb[:NE, 0:4], bank("pos")[:NE, NT * NE:NT * NE + 1].to_broadcast([NE, 4]), c_("thr")[:NE], ALU.is_gt))
            st.settle()
            v.sem_inc(s_freed("pos"), 1)
            st(red(xb[:NE, 4:5], xb[:NE, 0:4], ALU.add))
            st.settle()
            st(cp(xbb[:], xb[:NE, 4:5].to_broadcast([NE, P])))
            st.settle()
            v.sem_inc(xb_ready, 1)
            flat = lambda t: t.rearrange("p t e -> p (t e)")
            st(stt(flat(posm[:]), flat(posf[:]), 1.0, flat(msk[:]), ALU.add, ALU.mult))
            st.settle()
            st(ts(flat(posm[:]), flat(posm[:]), -1.0, None, ALU.add))
            v.wait_ge(*filled("xoff"))
            st(cp(xo[:], bank("xoff")[:, 0:2 * NE]))
            st.settle()
            v.sem_inc(s_freed("xoff"), 1)
            pg, pu, pd, px = unit
            def pick_rows(col):
                return tt(pick[:], iota.unsqueeze(1).to_broadcast([P, NT, P]), col.to_broadcast([P, NT, P]),
                          ALU.is_equal)

            def read_rows(n, col):
                v.wait_ge(tok_done, n + 1)
                with nc.allow_low_precision(reason="row numbers: whole and small"):
                    red(idx[:, col:col + 1], px[:, 0:2], ALU.add).then_inc(idx_ready, 1)

            pick_rows(posm[:, :, 0:1]).then_inc(picked, 1)
            st(ts(rowb[:], xo[:, 0:NE], float(NE - 1), float(P), ALU.add, ALU.mult))
            st.settle()
            st(tt(rowb[:], rowb[:], c_("eblock"), ALU.subtract))
            st(ts(flat(dmat[:]), flat(posf[:]), float(P), None, ALU.is_ge))
            st.settle()
            wide = lambda t: t.unsqueeze(1).to_broadcast([P, NT, NE])
            st(tt(dmat[:], dmat[:], wide(rowb[:]), ALU.mult))
            st(tt(posf[:], posf[:], wide(c_("eblock")), ALU.add))
            st.settle()
            read_rows(0, 0)
            v.wait_ge(tok_done, 1)
            pick_rows(posm[:, :, 1:2]).then_inc(picked, 1)
            st(tt(dmat[:], dmat[:], posf[:], ALU.add))
            st.settle()
            for i in range(NT):
                st(tt(dsel[:, i], onehot[:, i], dmat[:, i].unsqueeze(1).to_broadcast([P, TOPK, NE]), ALU.mult))
            st.settle()
            st(red(destf[:], dsel[:].rearrange("p t k e -> p (t k) e"), ALU.add))
            st.settle()
            st(cp(dest[:].rearrange("p t k -> p (t k)"), destf[:]))
            incl = xo[:, NE:2 * NE].unsqueeze(1).to_broadcast([P, MAXEXTRA, NE])
            st(tt(xle[:], incl, k_("jcol").unsqueeze(2).to_broadcast([P, MAXEXTRA, NE]), ALU.is_le))
            st.settle()
            st(tt(xlm[:], xle[:], incl, ALU.mult))
            st(red(exf[:, 0:MAXEXTRA], xle[:], ALU.add))
            st.settle()
            st(red(shift[:], xlm[:], ALU.max))
            st(cp(exf[:, MAXEXTRA:MAXEXTRA + 1], xo[:, 2 * NE - 1:2 * NE]))
            st.settle()
            st(tt(shift[:], k_("jcol"), shift[:], ALU.subtract))
            st.settle()
            st(ts(shift[:], shift[:], 1.0, float(P), ALU.add, ALU.mult))
            st(cp(itab[:], exf[:]))
            st.settle()
            v.sem_inc(routed, 1)

            pg, pu, pd, px = unit

            def rows_lo(n, par):
                v.wait_ge(xe_hi, n + 1)
                tt(xel[:, par].rearrange("p k s -> p (k s)"), px[:],
                   f(xeh[:, par]).rearrange("p k s -> p (k s)"), ALU.subtract).then_inc(xe_lo, 1)

            def gate_in(n, m_end):
                v.wait_ge(slot_used, m_end + S2)
                ts(gm[:], pg[:], LIMIT, None, ALU.min).then_inc(gate_read, 1)

            def gate_sig(n):
                v.wait_ge(sig2, n + 1)
                tt(sg[:], gm[:], sg[:], ALU.mult).then_inc(h_part, 1)

            v.wait_ge(x1_out, 16 * NT)
            rows_lo(0, 0)
            read_rows(1, 1)
            for j in range(EARLY_SPLIT, KD + AHEAD):
                lo_slot(0, j)
            rows_lo(1, 1)
            gate_in(0, KD)
            gate_sig(0)

            def dve_step(e, par, it=None, m0=None):
                last = isinstance(e, int) and e == NE - 1
                no_more = isinstance(e, int) and e >= NE - 2
                if not no_more:
                    v.wait_ge(tok_done, e + 2)
                    pick_rows(posm[:, :, bass.ds(e + 2, 1)]).then_inc(picked, 1)
                for j in range(AHEAD, 2 * KD if last else PER + AHEAD):
                    lo_slot(m0, j, it)
                    if j == (10 if last else 12):
                        v.wait_ge(slot_used, e * PER + 2 * KD + S2)
                        v.wait_ge(h_part, e * 2 + 1)
                        ts(hb[:], pu[:], -LIMIT, LIMIT, ALU.max, ALU.min).then_inc(h_part, 1)
                        v.wait_ge(h_part, e * 2 + 2)
                        stt(hb[:], hb[:], 1.0, sg[:], ALU.add, ALU.mult).then_inc(h_ready, 1)
                        if not no_more:
                            read_rows(e + 2, par)
                    if j == (12 if last else 18):
                        v.wait_ge(he_hi, e + 1)
                        tt(hel[:].rearrange("p k s -> p (k s)"), px[:], f(heh[:]).rearrange("p k s -> p (k s)"),
                           ALU.subtract).then_inc(he_lo, 1)
                    if j == 21:
                        gate_in(e + 1, (e + 1) * PER)
                    if j == 23:
                        gate_sig(e + 1)
                if not no_more:
                    rows_lo(e + 2, par)

            with v.Fori(0, NE // 2 - 1) as it:
                for par in range(2):
                    dve_step(it * 2 + par, par, it, KD + PER * par)
            for e in (NE - 2, NE - 1):
                dve_step(e, e % 2, None, KD + PER * e)

            n_extra = v.value_load(itab[0:1, MAXEXTRA:MAXEXTRA + 1], min_val=0, max_val=MAXEXTRA)
            v.wait_ge(y_stored, 16 * NE)
            v.wait_ge(ended, 1)
            with v.If(n_extra > 0):
                with v.Fori(0, MAXEXTRA) as j:
                    with v.If(j < n_extra):
                        ex = v.value_load(itab[0:1, bass.ds(j, 1)], min_val=0, max_val=NE - 1)
                        ts(xpos[:], posm[:, :, bass.ds(ex, 1)].rearrange("p n a -> p (n a)"),
                           shift[:, bass.ds(j, 1)], None, ALU.subtract).then_inc(v_hm, 1)
                        v.wait_ge(v_hm, j * 3 + 1)
                        pick_rows(xpos[:].unsqueeze(2)).then_inc(v_pick, 1)
                        v.wait_ge(v_tok, j + 1)
                        with nc.allow_low_precision(reason="row numbers: whole and small"):
                            red(eidx[:], px[:, 0:2], ALU.add).then_inc(v_idx, 1)
                        v.wait_ge(v_g, j + 1)
                        ts(gm[:], pg[:], LIMIT, None, ALU.min).then_inc(v_gm, 1)
                        v.wait_ge(v_sg, j + 1)
                        tt(sg[:], gm[:], sg[:], ALU.mult).then_inc(v_hm, 1)
                        v.wait_ge(v_u, j + 1)
                        ts(hb[:], pu[:], -LIMIT, LIMIT, ALU.max, ALU.min).then_inc(v_hm, 1)
                        v.wait_ge(v_hm, (j + 1) * 3)
                        stt(hb[:], hb[:], 1.0, sg[:], ALU.add, ALU.mult).then_inc(v_h, 1)
                        v.wait_ge(v_ysb, j + 1)
                        v.sem_inc(turn_over, 1)
            v.drain().then_inc(ended, 1)

            last = st

            def finish_norm(i):
                r = rows(i)
                v.wait_ge(std2, i + 1)
                last(nc.vector.reciprocal(rs2[:r, i:i + 1], rs2[:r, i:i + 1]))
                last.settle()
                last(stt(nmean2[:r, i:i + 1], mv2[:r, i, 0:1], -1.0, rs2[:r, i:i + 1], ALU.mult, ALU.mult), nmean_ready)

            for i in range(NT):
                r, b = rows(i), i % YB
                x_ = acc[:r, i]
                v.wait_ge(res_ready, i + 1)
                v.wait_ge(yk_in[b], 16 * TOPK * (i // YB + 1))
                for k in range(TOPK):
                    last(stt(x_, yk[:r, b, k], gate4[:r, i, k:k + 1], x_, ALU.mult, ALU.add))
                    last.settle()
                v.sem_inc(acc_read, 1)
                for h in range(2):
                    last(nc.vector.bn_stats(st2[:r, i, h], x_[:, h * HALF:(h + 1) * HALF]))
                last.settle()
                last(nc.vector.bn_aggr(mv2[:r, i], st2[:r, i].rearrange("p h s -> p (h s)")))
                last.settle()
                v.sem_inc(var2, 1)
                if i:
                    finish_norm(i - 1)
            finish_norm(NT - 1)


def constants():
    import numpy as np

    p = np.arange(P)
    keep_at, nkeep = offsets(KEEP)
    early_at, nearly = offsets(EARLY)
    keep, early = np.zeros((P, nkeep), np.float32), np.zeros((P, nearly), np.float32)

    def k(name):
        a, n = keep_at[name]
        return keep[:, a:a + n]

    def c(name):
        a, n = early_at[name]
        return early[:, a:a + n]

    k("ident")[:] = np.eye(P)
    k("iota")[:] = p[None]
    k("tokv")[:] = np.stack([np.broadcast_to(np.arange(NT) * P, (P, NT)),
                             np.broadcast_to(p[:, None], (P, NT))], -1).reshape(P, NT * 2)
    k("jcol")[:] = np.arange(MAXEXTRA)[None]
    s, t = p[:, None], p[None, :]
    c("cum")[:] = (s <= t) / 16.0
    c("rest")[:] = (s > t) / 16.0
    same = s // DEC == t // DEC
    c("cum_s")[:NS] = ((s <= t) & same)[:NS, :NS] / 16.0
    c("rest_s")[:NS] = ((s > t) & same)[:NS, :NS] / 16.0
    c("before")[:] = s < t
    c("ones")[:] = 1.0
    e = np.arange(NE)
    c("upto32")[:NE] = np.concatenate([e[:, None] < e[None], e[:, None] <= e[None]], 1)
    freqs = np.power(np.float32(500000.0), -np.arange(ROT, dtype=np.float32) * np.float32(2.0) / np.float32(2 * ROT))
    pos = np.zeros((P, NT), np.float32)
    pos[:, :PT] = np.arange(PT)[None] * P + p[:, None]
    pos[:NS, PT] = 2048 + np.arange(NS) % DEC
    ang = (pos[:, :, None] * freqs.astype(np.float32)).astype(np.float32)
    c("cos")[:] = np.cos(ang.astype(np.float64)).reshape(P, -1)
    c("sin")[:] = np.sin(ang.astype(np.float64)).reshape(P, -1)
    d = p[:, None] + W - np.arange(2 * W)[None]
    c("win")[:] = np.where((d >= 0) & (d < W), 0.0, NEG)
    nn, h, tok = p // 32, p // DEC % AH, p % DEC
    win_s = np.full((P, 2, NKEY), NEG, np.float32)
    sel = np.zeros((P, 2, AH, NS), np.float32)
    for b in range(2):
        n = b * 4 + nn
        win_s[:, b, :W] = np.where(np.arange(W)[None] > tok[:, None], 0.0, NEG)
        m = np.arange(NS)[None]
        win_s[:, b, W:] = np.where((m // DEC == n[:, None]) & (m % DEC <= tok[:, None]), 0.0, NEG)
        sel[p, b, h, n * DEC + tok] = 1.0
    c("win_s")[:] = win_s.reshape(P, -1)
    c("sel")[:] = sel.reshape(P, -1)
    c("half")[:] = (h // 4)[:, None] == np.arange(2)[None]
    for j, half in enumerate(LEVELS):
        at = np.arange(64)
        block = at // half
        c("level")[:, j * 64:(j + 1) * 64] = (s // (2 * half) == block[None]) & (s % (2 * half) < half)
        if half < DEC:
            block = np.arange(16) // half
            c("level_s")[:NS, (j - 5) * 16:(j - 4) * 16] = ((s // (2 * half) == block[None])
                                                            & (s % (2 * half) < half))[:NS]
    m = np.arange(NS)
    c("colseq")[:] = (m[None] // DEC == np.arange(NSEQ)[:, None]).reshape(1, -1)
    c("rowseq")[:] = p[:, None] // DEC == np.arange(NSEQ)[None]
    c("iota32")[:] = e[None]
    c("eblock")[:] = e[None] * P
    c("thr")[:] = np.arange(1, 5)[None] * P
    eident = np.concatenate([np.eye(NE)] * 2, 0).astype(np.float32)
    return keep, early, eident


_INS = ["x_prompt", "x_sample", "state_gla", "cache_swa_k", "cache_swa_v", "w_in", "w_gk_up", "b_gk_up",
        "gla_norm_g", "swa_sinks", "w_out", "ln1_g", "ln1_b", "w_router", "b_router", "w_gate", "b_gate",
        "w_up", "b_up", "w_down", "b_down", "ln2_g", "ln2_b"]
_OUTS = [("y_p", (1, SEQ, D)), ("y_s", (NSEQ, DEC, D)), ("st_p", (1, 1, GH, GDK, GDV)),
         ("st_s", (1, NSEQ, GH, GDK, GDV)), ("kp", (1, 1, W, KVH, HD)), ("vp", (1, 1, W, KVH, HD)),
         ("ks", (1, NSEQ, W, KVH, HD)), ("vs", (1, NSEQ, W, KVH, HD))]


def kernel(**inputs):
    import numpy as np
    import concourse.bacc as bacc
    from concourse.bass_utils import run_bass_kernel_spmd

    nc = bacc.Bacc("TRN2", target_bir_lowering=False, num_devices=1)
    arrays = {name: np.ascontiguousarray(inputs[name]) for name in _INS}
    arrays["keep"], arrays["early"], arrays["eident"] = constants()
    arrays["sinkrow"] = np.ascontiguousarray(np.tile(np.repeat(arrays["swa_sinks"][0], DEC), 4)[:, None])
    d = {}
    for name, a in arrays.items():
        d[name] = nc.dram_tensor(f"{name}_dram", a.shape, F32, kind="ExternalInput").ap()
    d["cache_k"], d["cache_v"] = d["cache_swa_k"], d["cache_swa_v"]
    for name, shape in _OUTS:
        d[name] = nc.dram_tensor(f"{name}_dram", shape, F32, kind="ExternalOutput").ap()
    build(nc, d)
    r = run_bass_kernel_spmd(nc, [{f"{name}_dram": a for name, a in arrays.items()}], core_ids=[0])
    return tuple(r.results[0][f"{name}_dram"] for name, _ in _OUTS)
```
